# Optimizing a Trainium2 kernel written in Bass

```python
import math
import functools
import jax
import jax.numpy as jnp
from jax import lax
import numpy as np

D_MODEL = 1024
BATCH = 1
SEQ = 256
DEPTH = 2

GRID_W = 64
CTX_LEN = 256
N_MIXERS = 2
N_HYENA = (DEPTH + N_MIXERS - 1) // N_MIXERS
N_MLSTM = DEPTH // N_MIXERS
N_SUB = 3
N_MOD = 3 * N_SUB
D_FF = 2816
NORM_EPS = 1e-6
POS_BASE = 10000.0
HY_ORDER = 2
HY_SHORT = 3
HY_EMB = 33
HY_BANDS = (HY_EMB - 1) // 2
HY_FILT_HIDDEN = 64
HY_DECAY_SLOW = -math.log(1e-2) / 1.5
HY_DECAY_FAST = -math.log(1e-2) / 0.3
ML_INNER = 2 * D_MODEL
ML_HEADS = 4
ML_HEAD_DIM = ML_INNER // ML_HEADS
ML_QKV_BLOCK = 4
ML_CONV = 3
ML_CHUNK = 64
ML_NORM_EPS = 1e-5
ML_FGATE_BIAS_LO = 3.0
ML_FGATE_BIAS_HI = 6.0

kernel_name = 'hyena_mlstm_macaron_dit'

def rms_norm(x, g):
    xf = x.astype(jnp.float32)
    y = xf * lax.rsqrt(jnp.mean(xf * xf, axis=-1, keepdims=True) + NORM_EPS)
    return (y * g.astype(jnp.float32)).astype(x.dtype)

def ada_chunks(cond, w, b):
    return jnp.split(jax.nn.silu(cond) @ w + b, N_MOD, axis=-1)

def ada_pre(h, g, shift, scale):
    return rms_norm(h, g) * (1.0 + scale) + shift

def swiglu(u, w_in, w_out):
    gate, val = jnp.split(u @ w_in, 2, axis=-1)
    return (jax.nn.silu(gate) * val) @ w_out

def conv_centred(x, w, b):
    width = w.shape[0]
    pad = width // 2
    n = x.shape[1]
    xp = jnp.pad(x, ((0, 0), (pad, pad), (0, 0)))
    return sum(xp[:, i:i + n] * w[i] for i in range(width)) + b

def pos_embed_2d(n_tokens, d, dtype):
    rows = n_tokens // GRID_W
    quarter = d // 4
    omega = 1.0 / (POS_BASE ** (jnp.arange(quarter, dtype=jnp.float32) / quarter))
    ang_r = jnp.arange(rows, dtype=jnp.float32)[:, None] * omega
    ang_c = jnp.arange(GRID_W, dtype=jnp.float32)[:, None] * omega
    row_emb = jnp.concatenate([jnp.sin(ang_r), jnp.cos(ang_r)], axis=-1)
    col_emb = jnp.concatenate([jnp.sin(ang_c), jnp.cos(ang_c)], axis=-1)
    emb = jnp.concatenate([
        jnp.broadcast_to(row_emb[:, None, :], (rows, GRID_W, d // 2)),
        jnp.broadcast_to(col_emb[None, :, :], (rows, GRID_W, d // 2))], axis=-1)
    return emb.reshape(rows * GRID_W, d).astype(dtype)

def hyena_filters(n, f_w1, f_b1, f_w2, f_b2, f_w3, f_b3, f_freq, log_decay):
    f32 = jnp.float32
    d = log_decay.shape[-1]
    t = jnp.arange(n, dtype=f32)
    t_norm = t / max(n - 1, 1)
    bands = jnp.linspace(1e-4, HY_BANDS - 1, HY_BANDS, dtype=f32)
    ang = ((2.0 * math.pi / n) * t)[:, None] * bands[None, :]
    feats = jnp.concatenate([t_norm[:, None], jnp.cos(ang), -jnp.sin(ang)], axis=-1)
    h = jnp.sin(f_freq[0].astype(f32) * (feats @ f_w1.astype(f32) + f_b1.astype(f32)))
    h = jnp.sin(f_freq[1].astype(f32) * (h @ f_w2.astype(f32) + f_b2.astype(f32)))
    h = (h @ f_w3.astype(f32) + f_b3.astype(f32)).reshape(n, HY_ORDER, 2, d)
    h = h.transpose(1, 2, 0, 3)
    window = jnp.exp(-t_norm[None, None, :, None] * jnp.exp(log_decay.astype(f32))[:, :, None, :])
    h = h * window
    fwd = h[:, 0]
    bwd = h[:, 1, 1:][:, ::-1]
    k = jnp.concatenate([fwd, jnp.zeros((HY_ORDER, 1, d), f32), bwd], axis=1)
    return k * lax.rsqrt(jnp.sum(k * k, axis=1, keepdims=True) + 1e-12)

def long_conv(z, k_freq, skip):
    n = z.shape[1]
    zf = jnp.fft.rfft(z, n=2 * n, axis=1)
    y = jnp.fft.irfft(zf * k_freq[None], n=2 * n, axis=1)[:, :n]
    return y + z * skip.astype(jnp.float32)

def hyena_mixer(u, w_in, b_in, conv_w, conv_b, f_w1, f_b1, f_w2, f_b2, f_w3, f_b3,
                f_freq, log_decay, skip, w_out, b_out):
    n = u.shape[1]
    proj = conv_centred(u @ w_in + b_in, conv_w, conv_b).astype(jnp.float32)
    x1, x2, v = jnp.split(proj, 3, axis=-1)
    k = hyena_filters(n, f_w1, f_b1, f_w2, f_b2, f_w3, f_b3, f_freq, log_decay)
    k_freq = jnp.fft.rfft(k, axis=1)
    z = x1 * long_conv(v, k_freq[0], skip[0])
    z = x2 * long_conv(z, k_freq[1], skip[1])
    return z.astype(u.dtype) @ w_out + b_out

def blockdiag(x, w):
    bsz, n, ch = x.shape
    nb, bs, _ = w.shape
    return jnp.einsum('blnd,nde->blne', x.reshape(bsz, n, nb, bs), w).reshape(bsz, n, ch)

def mlstm_scan(q, k, v, i_pre, f_pre):
    bsz, n, nh, dh = q.shape
    n_chunks = n // ML_CHUNK

    def chunks(a):
        a = a.reshape(bsz, n_chunks, ML_CHUNK, nh, *a.shape[3:])
        return jnp.moveaxis(a, (1, 3), (0, 2))

    log_f = jax.nn.log_sigmoid(f_pre)
    mask = jnp.tril(jnp.ones((ML_CHUNK, ML_CHUNK), dtype=bool))

    def step(carry, inp):
        c_st, n_st, m_st = carry
        qc, kc, vc, ic, lfc = inp
        b = jnp.cumsum(lfc, axis=-1)
        a = b + m_st[..., None]
        dmat = jnp.where(mask, b[..., :, None] - b[..., None, :] + ic[..., None, :], -jnp.inf)
        m_j = jnp.maximum(a, jnp.max(dmat, axis=-1))
        w_inter = jnp.exp(a - m_j)
        s = jnp.einsum('bhjd,bhsd->bhjs', qc, kc) * jnp.exp(dmat - m_j[..., None])
        num = w_inter[..., None] * jnp.einsum('bhjd,bhde->bhje', qc, c_st) + jnp.einsum('bhjs,bhse->bhje', s, vc)
        qn = w_inter * jnp.einsum('bhjd,bhd->bhj', qc, n_st) + jnp.sum(s, axis=-1)
        h = num / jnp.maximum(jnp.abs(qn), jnp.exp(-m_j))[..., None]
        b_last = b[..., -1]
        g = b_last[..., None] - b + ic
        m_new = jnp.maximum(b_last + m_st, jnp.max(g, axis=-1))
        decay = jnp.exp(b_last + m_st - m_new)
        kw = kc * jnp.exp(g - m_new[..., None])[..., None]
        c_new = decay[..., None, None] * c_st + jnp.einsum('bhsd,bhse->bhde', kw, vc)
        n_new = decay[..., None] * n_st + jnp.sum(kw, axis=-2)
        return (c_new, n_new, m_new), h

    f32 = jnp.float32
    init = (jnp.zeros((bsz, nh, dh, dh), f32), jnp.zeros((bsz, nh, dh), f32), jnp.zeros((bsz, nh), f32))
    _, h = lax.scan(step, init, (chunks(q), chunks(k), chunks(v), chunks(i_pre), chunks(log_f)))
    return jnp.moveaxis(h, (0, 2), (1, 3)).reshape(bsz, n, nh, dh)

def mlstm_mixer(u_ctx, u_lat, w_up, conv_w, conv_b, w_q, w_k, w_v, w_gate, b_gate,
                norm_g, skip, w_down, with_ctx_out):
    n_ctx = u_ctx.shape[1]

    def branch(u):
        xm, z = jnp.split(u @ w_up, 2, axis=-1)
        xc = jax.nn.silu(conv_centred(xm, conv_w, conv_b))
        q = blockdiag(xc, w_q)
        k = blockdiag(xc, w_k)
        v = blockdiag(xm, w_v)
        gates = jnp.concatenate([q, k, v], axis=-1) @ w_gate + b_gate
        return xc, z, q, k, v, gates

    xc, z, q, k, v, gates = [jnp.concatenate([pc, pl], axis=1)
                             for pc, pl in zip(branch(u_ctx), branch(u_lat))]
    bsz, n, _ = q.shape

    def heads(a):
        return a.astype(jnp.float32).reshape(bsz, n, ML_HEADS, ML_HEAD_DIM)

    q, k, v = heads(q), heads(k) * (ML_HEAD_DIM ** -0.5), heads(v)
    gates = gates.astype(jnp.float32).reshape(bsz, n, 2, 2, ML_HEADS)

    def rev(a):
        return jnp.concatenate([a[:, :n_ctx][:, ::-1], a[:, n_ctx:][:, ::-1]], axis=1)

    h_fwd = mlstm_scan(q, k, v, gates[:, :, 0, 0], gates[:, :, 0, 1])
    h_bwd = rev(mlstm_scan(rev(q), rev(k), rev(v), rev(gates[:, :, 1, 0]), rev(gates[:, :, 1, 1])))
    h = h_fwd + h_bwd
    mu = jnp.mean(h, axis=-1, keepdims=True)
    var = jnp.mean(jnp.square(h - mu), axis=-1, keepdims=True)
    h = ((h - mu) * lax.rsqrt(var + ML_NORM_EPS)).reshape(bsz, n, ML_INNER) * norm_g.astype(jnp.float32)
    h = (h.astype(u_lat.dtype) + skip * xc) * jax.nn.silu(z)
    y_lat = h[:, n_ctx:] @ w_down
    y_ctx = h[:, :n_ctx] @ w_down if with_ctx_out else None
    return y_ctx, y_lat

def setup_inputs(seed: int = 0) -> dict:
    key = jax.random.key(seed)
    ks = iter(jax.random.split(key, 48))
    f32 = jnp.float32

    def nrm(shape, scale):
        return jax.random.normal(next(ks), shape, f32) * scale

    d, ff, inner, nh, qb, fh = D_MODEL, D_FF, ML_INNER, ML_HEADS, ML_QKV_BLOCK, HY_FILT_HIDDEN
    i_bias = nrm((N_MLSTM, 2, 1, nh), 0.1)
    f_bias = jax.random.uniform(next(ks), (N_MLSTM, 2, 1, nh), f32, ML_FGATE_BIAS_LO, ML_FGATE_BIAS_HI)
    return {
        'x': nrm((BATCH, SEQ, d), 1.0),
        'c': nrm((BATCH, d), 1.0),
        'ctx': nrm((BATCH, CTX_LEN, d), 1.0),
        'c_ctx': nrm((d,), 1.0),
        'ada_w': nrm((DEPTH, d, N_MOD * d), 0.5 * d ** -0.5),
        'ada_b': nrm((DEPTH, N_MOD * d), 0.01),
        'norm_g': 1.0 + nrm((DEPTH, N_SUB, d), 0.02),
        'final_g': 1.0 + nrm((d,), 0.02),
        'ffn_w_in': nrm((DEPTH, 2, d, 2 * ff), d ** -0.5),
        'ffn_w_out': nrm((DEPTH, 2, ff, d), ff ** -0.5),
        'hy_w_in': nrm((N_HYENA, d, 3 * d), d ** -0.5),
        'hy_b_in': nrm((N_HYENA, 3 * d), 0.01),
        'hy_conv_w': nrm((N_HYENA, HY_SHORT, 3 * d), HY_SHORT ** -0.5),
        'hy_conv_b': nrm((N_HYENA, 3 * d), 0.01),
        'hy_f_w1': nrm((N_HYENA, HY_EMB, fh), HY_EMB ** -0.5),
        'hy_f_b1': nrm((N_HYENA, fh), 0.01),
        'hy_f_w2': nrm((N_HYENA, fh, fh), fh ** -0.5),
        'hy_f_b2': nrm((N_HYENA, fh), 0.01),
        'hy_f_w3': nrm((N_HYENA, fh, HY_ORDER * 2 * d), fh ** -0.5),
        'hy_f_b3': nrm((N_HYENA, HY_ORDER * 2 * d), 0.01),
        'hy_f_freq': 1.0 + nrm((N_HYENA, 2, fh), 0.02),
        'hy_log_decay': jax.random.uniform(next(ks), (N_HYENA, HY_ORDER, 2, d), f32,
                                           math.log(HY_DECAY_SLOW), math.log(HY_DECAY_FAST)),
        'hy_skip': nrm((N_HYENA, HY_ORDER, d), 0.5),
        'hy_w_out': nrm((N_HYENA, d, d), d ** -0.5),
        'hy_b_out': nrm((N_HYENA, d), 0.01),
        'ml_w_up': nrm((N_MLSTM, d, 2 * inner), d ** -0.5),
        'ml_conv_w': nrm((N_MLSTM, ML_CONV, inner), ML_CONV ** -0.5),
        'ml_conv_b': nrm((N_MLSTM, inner), 0.01),
        'ml_w_q': nrm((N_MLSTM, inner // qb, qb, qb), qb ** -0.5),
        'ml_w_k': nrm((N_MLSTM, inner // qb, qb, qb), qb ** -0.5),
        'ml_w_v': nrm((N_MLSTM, inner // qb, qb, qb), qb ** -0.5),
        'ml_w_gate': nrm((N_MLSTM, 3 * inner, 4 * nh), 0.1 * (3 * inner) ** -0.5),
        'ml_b_gate': jnp.concatenate([i_bias, f_bias], axis=2).reshape(N_MLSTM, 4 * nh),
        'ml_norm_g': 1.0 + nrm((N_MLSTM, inner), 0.02),
        'ml_skip': 1.0 + nrm((N_MLSTM, inner), 0.02),
        'ml_w_down': nrm((N_MLSTM, inner, d), inner ** -0.5),
    }

def reference(x, c, ctx, c_ctx, ada_w, ada_b, norm_g, final_g, ffn_w_in, ffn_w_out,
              hy_w_in, hy_b_in, hy_conv_w, hy_conv_b, hy_f_w1, hy_f_b1, hy_f_w2, hy_f_b2,
              hy_f_w3, hy_f_b3, hy_f_freq, hy_log_decay, hy_skip, hy_w_out, hy_b_out,
              ml_w_up, ml_conv_w, ml_conv_b, ml_w_q, ml_w_k, ml_w_v, ml_w_gate, ml_b_gate,
              ml_norm_g, ml_skip, ml_w_down):
    n_lat = x.shape[1]
    h_lat = x + pos_embed_2d(n_lat, x.shape[-1], x.dtype)[None]
    h_ctx = ctx
    for l in range(DEPTH):
        last = l == DEPTH - 1
        j = l // N_MIXERS
        m_lat = [m[:, None, :] for m in ada_chunks(c, ada_w[l], ada_b[l])]
        m_ctx = ada_chunks(c_ctx, ada_w[l], ada_b[l])
        h_lat = h_lat + 0.5 * m_lat[2] * swiglu(ada_pre(h_lat, norm_g[l, 0], m_lat[0], m_lat[1]),
                                                ffn_w_in[l, 0], ffn_w_out[l, 0])
        h_ctx = h_ctx + 0.5 * m_ctx[2] * swiglu(ada_pre(h_ctx, norm_g[l, 0], m_ctx[0], m_ctx[1]),
                                                ffn_w_in[l, 0], ffn_w_out[l, 0])
        u_lat = ada_pre(h_lat, norm_g[l, 1], m_lat[3], m_lat[4])
        u_ctx = ada_pre(h_ctx, norm_g[l, 1], m_ctx[3], m_ctx[4])
        if l % N_MIXERS == 0:
            hy = functools.partial(
                hyena_mixer, w_in=hy_w_in[j], b_in=hy_b_in[j], conv_w=hy_conv_w[j], conv_b=hy_conv_b[j],
                f_w1=hy_f_w1[j], f_b1=hy_f_b1[j], f_w2=hy_f_w2[j], f_b2=hy_f_b2[j], f_w3=hy_f_w3[j],
                f_b3=hy_f_b3[j], f_freq=hy_f_freq[j], log_decay=hy_log_decay[j], skip=hy_skip[j],
                w_out=hy_w_out[j], b_out=hy_b_out[j])
            y_lat = hy(u_lat)
            y_ctx = None if last else hy(u_ctx)
        else:
            y_ctx, y_lat = mlstm_mixer(u_ctx, u_lat, ml_w_up[j], ml_conv_w[j], ml_conv_b[j], ml_w_q[j],
                                       ml_w_k[j], ml_w_v[j], ml_w_gate[j], ml_b_gate[j], ml_norm_g[j],
                                       ml_skip[j], ml_w_down[j], with_ctx_out=not last)
        h_lat = h_lat + m_lat[5] * y_lat
        h_lat = h_lat + 0.5 * m_lat[8] * swiglu(ada_pre(h_lat, norm_g[l, 2], m_lat[6], m_lat[7]),
                                                ffn_w_in[l, 1], ffn_w_out[l, 1])
        if not last:
            h_ctx = h_ctx + m_ctx[5] * y_ctx
            h_ctx = h_ctx + 0.5 * m_ctx[8] * swiglu(ada_pre(h_ctx, norm_g[l, 2], m_ctx[6], m_ctx[7]),
                                                    ffn_w_in[l, 1], ffn_w_out[l, 1])
    return rms_norm(h_lat, final_g)


_drawn_inputs = setup_inputs


def setup_inputs(seed=0):
    import zlib

    import numpy as np

    out = dict(_drawn_inputs(seed))
    spreads = {}
    factors = {'final_g': 20.425,
     'hy_b_in': 3.175,
     'hy_conv_b': 3.71,
     'hy_f_freq': 2.97,
     'hy_b_out': 8.0,
     'ml_conv_b': 8.0,
     'ml_w_gate': 8.0,
     'ml_norm_g': 130.189,
     'ml_skip': 200.0}
    for name, (base, spread) in spreads.items():
        noise = np.random.default_rng([zlib.crc32(name.encode()), seed]).standard_normal(out[name].shape)
        drawn = base * np.exp(spread * noise) if base else spread * noise
        out[name] = jnp.asarray(drawn.astype(out[name].dtype))
    for name, factor in factors.items():
        out[name] = (out[name] * factor).astype(out[name].dtype)
    return out
```

```python
import math
from contextlib import ExitStack

import numpy as np

import concourse.bass as bass
from concourse import mybir

F32 = mybir.dt.float32
F32R = mybir.dt.float32r
ALU = mybir.AluOpType
ACT = mybir.ActivationFunctionType

P = 128
D = 1024
KT = D // P
CTX = 256
LAT = 256
TOK = CTX + LAT
FF = 2816
FT = FF // P
NFI = FF // 256
NFO = FT // 2
BLK = 2048
INNER = 2 * D
HEADS = 4
DH = INNER // HEADS
HT = DH // P
IT = INNER // P
FILT = 64
EMB = 33
BANDS = (EMB - 1) // 2
NSUB = 6
ADA_PAIRS = 6
ALLC, LATC = slice(0, TOK), slice(CTX, TOK)
SEQS = ((slice(0, CTX), 0), (slice(CTX, TOK), 1))

G_FFN = [0, 49, 82, 139]
G_HYIN, G_HYOUT, G_MLUP, G_MLDN = 33, 45, 115, 131
N_BLOCKS = 172


def column_places():
    at, n = {}, 0
    for name, k in (("norm_g", 48), ("final_g", 8), ("hy_b_in", 24), ("hy_conv_w", 72), ("hy_conv_b", 24),
                    ("hy_skip", 16), ("hy_b_out", 8), ("ml_conv_w", 48), ("ml_conv_b", 16), ("ml_norm_g", 16),
                    ("ml_skip", 16), ("ada_b", 144), ("cond", 16), ("f_freq", 2), ("f_b1", 1), ("f_b2", 1),
                    ("b_gate", 4), ("mean_w", 1), ("eps_norm", 1), ("eps_ml", 1), ("eps_filt", 1),
                    ("neg_t", 2), ("tap_mask", 2), ("one", 1), ("cond_sel", 2)):
        at[name] = n
        n += k
    return at, n


def build(nc, dram):
    at, n_vec = column_places()
    with ExitStack() as ctx:
        place = [-(-nc.sbuf_base // 64) * 64]

        def fixed(name, shape, dt=F32):
            n = int(np.prod(shape[1:])) * 4
            t = nc.alloc_sbuf_tensor_at(name, shape, dt, offset=place[0])
            place[0] += -(-n // 32) * 32
            return t

        def over(name, shape, offset, dt=F32):
            return nc.alloc_sbuf_tensor_at(name, shape, dt, offset=offset)

        def sem(name):
            return ctx.enter_context(nc.semaphore(name))

        h = fixed("h", [P, KT, TOK])
        act_at = place[0]
        act_hi = fixed("act_hi", [P, KT, TOK], F32R)
        act_lo = fixed("act_lo", [P, KT, TOK], F32R)
        w_raw = fixed("w_raw", [P, 2, BLK])
        w_hi = fixed("w_hi", [P, 2, BLK], F32R)
        w_lo = fixed("w_lo", [P, 2, BLK], F32R)
        ada_at = place[0]
        ada_raw = fixed("ada_raw", [P, 2, KT, 256])
        scr_at = place[0]
        scratch = fixed("scratch", [P, 24, TOK])
        tmp_at = place[0]
        place[0] += 8192
        kst_at = place[0]
        place[0] += 32768
        vec = fixed("vec", [P, n_vec])
        mods = fixed("mods", [P, 144, 2])
        coef_a = fixed("coef_a", [P, NSUB, KT, 2])
        coef_g = fixed("coef_g", [P, NSUB, KT, 2])
        ident = fixed("ident", [P, P])
        ones = fixed("ones", [P, P])
        cond_pad = fixed("cond_pad", [P, KT, 32])
        w_comb = fixed("w_comb", [P, IT, 2, 16])
        cols4 = fixed("cols4", [P, 2, 4])
        rnorm = fixed("rnorm", [P, 2, KT])
        assert place[0] <= nc.sbuf_usable_end, place[0] - nc.sbuf_usable_end

        def col(name, i=0, n=1):
            return vec[:, at[name] + i:at[name] + i + n]

        hidden = scratch
        silu_g = over("silu_g", [P, 2, TOK], tmp_at)
        ada_part = over("ada_part", [P, 512], tmp_at + 4096)
        nrm = scr_at + 32768
        tn = over("tn", [P, 2, TOK], nrm)
        uf = over("uf", [P, 2, TOK], nrm + 4096)
        sq = over("sq", [P, 2, TOK], nrm + 8192)
        diag = over("diag", [P, 4, P], nrm + 12288)
        w3aug = over("w3aug", [P, 4096], scr_at)
        edecay = over("edecay", [P, 4096], scr_at + 16384)
        pos = over("pos", [P, KT, LAT], scr_at + 32768)
        window = over("window", [P, 2, 2, 512], scr_at + 40960)
        dft_f = over("dft_f", [P, 2, 2, 256], act_at)
        fk = over("fk", [P, 2, 2, 512], act_at + 4096)
        fsd = over("fsd", [P, 2, 2, 512], act_at + 12288)
        fsq = over("fsq", [P, 2, 2, 512], act_at + 20480)
        fmlp = over("fmlp", [P, 4, 256], act_at + 28672)
        fsmall = over("fsmall", [P, 384], tmp_at)
        kst = over("kst", [P, 2, 4, D], kst_at)
        hyp = scratch
        pad = over("pad", [P, 2, 2, 258], tmp_at)
        dft_h = over("dft_h", [P, 2, 2, 256], act_at + 24576)
        dft_i = over("dft_i", [P, 2, 2, 256], act_at + 28672)
        zt = over("zt", [P, 2, 2, 512], act_at)
        zf = over("zf", [P, 2, 4, 512], act_at + 8192)
        pwa = over("pwa", [P, 2, 512], tmp_at)
        gate_t = over("gate_t", [P, 4, 256], tmp_at)
        pwb = over("pwb", [P, 2, 512], tmp_at + 4096)
        bdt = over("bdt", [P, 3, IT, P], kst_at)
        wg = over("wg", [P, 3, IT, 16], kst_at + 24576)
        v_tok = over("v_tok", [P, 4, INNER], kst_at)
        score = over("score", [P, HEADS, 2, TOK], scr_at)
        xs = over("xs", [P, IT, LAT], scr_at + 16384)
        k_head = over("k_head", [P, HT, TOK], scr_at + 32768)
        q_head = over("q_head", [P, HT, LAT], scr_at + 40960)
        xc = over("xc", [P, 2, TOK], scr_at + 45056)
        bd = over("bd", [P, 2, HT, 3, P], ada_at)
        zs = over("zs", [P, IT, LAT], scr_at + 32768)
        row_i = over("row_i", [P, 2, TOK], tmp_at)
        row_f = over("row_f", [P, 2, TOK], tmp_at + 4096)
        row_c = over("row_c", [P, 2, TOK], ada_at)
        row_d = over("row_d", [P, 2, TOK], ada_at + 4096)
        row_e = over("row_e", [P, 2, TOK], ada_at + 8192)
        row_g = over("row_g", [P, 2, TOK], ada_at + 12288)
        gsum = over("gsum", [P, TOK], ada_at + 12288)
        mask = over("mask", [P, 2, 2, LAT], act_at)
        pd = over("pd", [P, 2, TOK], act_at + 4096)
        ht = [over(f"ht{j}", [P, INNER], act_at + 8192 + 16384 * j) for j in range(2)]
        pt = over("pt", [P, 2, 4, P], act_at + 16384)
        pc = over("pc", [P, TOK], act_at + 20480)
        acols = over("acols", [P, 256], act_at + 22528)
        ym = over("ym", [P, IT, LAT], scr_at)
        out_sb = over("out_sb", [P, KT, LAT], scr_at)

        ps = ctx.enter_context(nc.psum_tensor("ps", [P, 8, 512], F32))

        s_const, s_w3, s_tok, s_pos = sem("const_loaded"), sem("filter_in_loaded"), sem("tokens_loaded"), sem("pos_loaded")
        s_dft, s_bdt, s_mask, s_out = sem("dft_loaded"), sem("gate_w_loaded"), sem("mask_loaded"), sem("out_stored")
        w_loaded = [sem("w_loaded0"), sem("w_loaded1")]
        w_hi_done, w_lo_done, w_used = sem("w_hi_done"), sem("w_lo_done"), sem("w_used")
        ada_loaded = [sem("ada_loaded0"), sem("ada_loaded1")]
        ada_used, ada_evac, ada_cols, ada_mods = sem("ada_used"), sem("ada_evac"), sem("ada_cols"), sem("ada_mods")
        cond_zero, cond_ready = sem("cond_zero"), sem("cond_ready")
        h_ready, sq_ready, ss_done, std_ready = sem("h_ready"), sem("sq_ready"), sem("ss_done"), sem("std_ready")
        rstd_ready, diag_ready, rb_ready = sem("rstd_ready"), sem("diag_ready"), sem("rb_ready")
        tn_ready, uf_ready, uhi_ready, u_ready = sem("tn_ready"), sem("uf_ready"), sem("uhi_ready"), sem("u_ready")
        coef_ready, silu_done, mul_done = sem("coef_ready"), sem("silu_done"), sem("mul_done")
        in_hi, in_lo, y_done = sem("in_hi"), sem("in_lo"), sem("y_done")
        f_pe, f_act, f_dve = sem("filter_pe"), sem("filter_act"), sem("filter_dve")
        pad_zero, pad_ready, conv_step = sem("pad_zero"), sem("pad_ready"), sem("conv_step")
        t_done, t_evac, fwd_done, fwd_evac = sem("t_done"), sem("t_evac"), sem("fwd_done"), sem("fwd_evac")
        pw_done, inv_done, z_done, hy_step = sem("pw_done"), sem("inv_done"), sem("z_done"), sem("hy_step")
        comb_done, comb_ready = sem("comb_done"), sem("comb_ready")
        bd_loaded = [sem("bd_loaded0"), sem("bd_loaded1")]
        xm_ready, xc_step, xc_ready, xs_done = sem("xm_ready"), sem("xc_step"), sem("xc_ready"), sem("xs_done")
        kq_done, kq_evac, v_done, v_evac, qkv_done = (
            sem("kq_done"), sem("kq_evac"), sem("v_done"), sem("v_evac"), sem("qkv_done"))
        sc_done, sc_evac, z_evac = sem("sc_done"), sem("sc_evac"), sem("z_evac")
        sel_done, row_act, row_dve = sem("sel_done"), sem("row_act"), sem("row_dve")
        rcol_done, rcol_ready, bc_done, a_dve, a_exp = (
            sem("rcol_done"), sem("rcol_ready"), sem("bc_done"), sem("a_dve"), sem("a_exp"))
        pt_done, pt_evac, pv_done, pv_evac, stat_done = (
            sem("pt_done"), sem("pt_evac"), sem("pv_done"), sem("pv_evac"), sem("stat_done"))
        hn_std, hn_ready, hnt_done, ym_step = sem("hn_std"), sem("hn_ready"), sem("hnt_done"), sem("ym_step")
        out_ready = sem("out_ready")

        IN_BEFORE = [0, 11, 15, 26, 37, 45]
        OUT_BLOCKS = [G_FFN[0] + 22, G_HYOUT, G_FFN[1] + 22, G_FFN[2] + 22, G_MLDN, G_FFN[3] + 22]
        OUT_N = [NFO, 4, NFO, NFO, 8, NFO]
        ROW = {s: i + 1 for i, s in enumerate(
            ("zero", "gsum0", "gsum1", "i0", "f0", "i1", "f1", "lf", "cum0", "cum1", "cum2", "cum3", "g",
             "max0", "max1", "max2", "max3", "m"))}
        A_STEPS = 11
        R = slice(0, HEADS)

        block = ctx.enter_context(nc.Block())

        @block.sync
        def _(sp):
            def load_w(g, i=0):
                if g >= 2:
                    sp.wait_ge(w_lo_done, g - 1 + 2 * i)
                src = dram["w_stream"][g] if isinstance(i, int) else \
                    dram["w_stream"][bass.ds(g + 2 * i, 1)].rearrange("a p n -> (a p) n")
                sp.dma_start(w_raw[:, g % 2, :], src).then_inc(w_loaded[g % 2], 16)

            def load_pairs(g, n):
                with sp.Fori(0, n) as i:
                    load_w(g, i)
                    load_w(g + 1, i)

            sp.dma_start(vec[:], dram["vec"]).then_inc(s_const, 16)
            sp.dma_start(ident[:], dram["ident"]).then_inc(s_const, 16)
            sp.dma_start(ones[:], dram["ones"]).then_inc(s_const, 16)
            sp.dma_start(fsmall[:], dram["fsmall"]).then_inc(s_w3, 16)
            sp.dma_start(dft_f[:], dram["dft_f"]).then_inc(s_w3, 16)
            sp.dma_start(w3aug[0:FILT + 1, :], dram["w3aug"]).then_inc(s_w3, 16)
            sp.dma_start(edecay[:], dram["log_decay"].to_broadcast([P, 4096])).then_inc(s_w3, 16)
            sp.dma_start(h[:], dram["tokens"]).then_inc(s_tok, 16)
            sp.dma_start(pos[:], dram["pos"]).then_inc(s_pos, 16)
            load_w(0)
            load_w(1)
            load_pairs(2, 22)
            load_w(46)
            sp.wait_ge(w_used, G_HYOUT)
            sp.dma_start(dft_h[:], dram["dft_f"]).then_inc(s_dft, 16)
            sp.dma_start(dft_i[:], dram["dft_i"]).then_inc(s_dft, 16)
            load_w(47)
            load_w(48)
            sp.wait_ge(pw_done, 8)
            sp.dma_start(bdt[:], dram["bdt"]).then_inc(s_bdt, 16)
            sp.dma_start(wg[:], dram["wg"]).then_inc(s_bdt, 16)
            load_pairs(49, 33)
            sp.wait_ge(ada_used, 2 * ADA_PAIRS * NSUB)
            sp.dma_start(bd[:, 0], dram["bd"][0]).then_inc(bd_loaded[0], 16)
            sp.dma_start(bd[:, 1], dram["bd"][1]).then_inc(bd_loaded[1], 16)
            for g in range(115, 121):
                load_w(g)
            sp.wait_ge(qkv_done, 4)
            sp.dma_start(bd[:, 0], dram["bd"][2]).then_inc(bd_loaded[0], 16)
            for g in range(121, 124):
                load_w(g)
            sp.wait_ge(qkv_done, 8)
            sp.dma_start(bd[:, 1], dram["bd"][3]).then_inc(bd_loaded[1], 16)
            load_pairs(124, 4)
            load_w(132)
            sp.wait_ge(w_used, G_MLDN)
            sp.dma_start(mask[:], dram["mask"]).then_inc(s_mask, 16)
            load_pairs(133, 19)
            load_w(171)
            sp.wait_ge(out_ready, KT)
            sp.dma_start(dram["out"], out_sb[:]).then_inc(s_out, 16)
            sp.wait_ge(s_out, 16)

        @block.gpsimd
        def _(pool):
            for s in range(2):
                pool.dma_start(ada_raw[:, s], dram["ada_stream"][s]).then_inc(ada_loaded[s], 16)
            with pool.Fori(1, ADA_PAIRS * NSUB) as q:
                for s in range(2):
                    pool.wait_ge(ada_used, 2 * q - 1 + s)
                    pool.dma_start(ada_raw[:, s],
                                   dram["ada_stream"][bass.ds(2 * q + s, 1)].rearrange("a p k n -> (a p) k n")
                                   ).then_inc(ada_loaded[s], 16)

        @block.scalar
        def _(act):
            def split_w(g, i=0):
                if g >= N_BLOCKS:
                    return
                act.wait_ge(w_loaded[g % 2], 16 * (g // 2 + 1) + 16 * i)
                if g >= 2:
                    act.wait_ge(w_used, g - 1 + 2 * i)
                act.activation(w_hi[:, g % 2, :], w_raw[:, g % 2, :], ACT.Copy).then_inc(w_hi_done, 1)

            def squares(n, cols):
                for m in range(KT):
                    act.wait_ge(h_ready, 8 * n + m + 1)
                    if m >= 2:
                        act.wait_ge(ss_done, 8 * n + m - 1)
                    act.activation(sq[:, m % 2, cols], h[:, m, cols], ACT.Square).then_inc(sq_ready, 1)
                w = (cols.stop - cols.start) // P
                act.wait_ge(ss_done, 8 * n + KT)
                act.activation(cols4[:, 0, 0:w], ps[:, 0, 0:w], ACT.Sqrt, bias=col("eps_norm")).then_inc(std_ready, 1)

            def affine(n, cols):
                act.wait_ge(coef_ready, 2 * n + 2)
                for k in range(KT):
                    act.wait_ge(tn_ready, 8 * n + k + 1)
                    if k >= 2:
                        act.wait_ge(u_ready, 8 * n + k - 1)
                    for c, cd in SEQS:
                        if c.start >= cols.start:
                            last = act.activation(uf[:, k % 2, c], tn[:, k % 2, c], ACT.Identity,
                                                  scale=coef_a[:, n, k, cd:cd + 1],
                                                  bias=mods[:, 24 * n + k, cd:cd + 1])
                    last.then_inc(uf_ready, 1)
                    act.wait_ge(uf_ready, 8 * n + k + 1)
                    act.activation(act_hi[:, k, cols], uf[:, k % 2, cols], ACT.Copy).then_inc(uhi_ready, 1)

            def ffn_in(f, cols):
                g0 = G_FFN[f]

                def step(p, i=0):
                    if p > 0 or f > 0:
                        act.wait_ge(mul_done, NFI * f + p + i)
                    act.wait_ge(w_used, g0 + 2 * p + 1 + 2 * i)
                    act.activation(silu_g[:, :, cols], ps[:, 0:2, cols], ACT.Silu).then_inc(silu_done, 1)
                    split_w(g0 + 2 * p + 2, i)
                    split_w(g0 + 2 * p + 3, i)

                step(0)
                with act.Fori(0, NFI - 1) as i:
                    step(1, i)

            def out_proj(o, cols, src, first_ready):
                g0, nb = OUT_BLOCKS[o], OUT_N[o]

                def split_in(b, i=0):
                    if b < 2:
                        first_ready(act, b)
                    else:
                        act.wait_ge(w_used, g0 + b - 1 + 2 * i)
                    s = 2 * (b % 2)
                    act.activation(act_hi[:, s:s + 2, cols], src(b, i), ACT.Copy).then_inc(in_hi, 1)

                def step(b, i=0):
                    split_w(g0 + b + 2, i)
                    if b + 2 < nb:
                        split_in(b + 2, i)

                split_in(0)
                split_in(1)
                loops = (nb - 3) // 2
                if loops:
                    with act.Fori(0, loops) as i:
                        step(0, i)
                        step(1, i)
                for b in range(2 * loops, nb - 1):
                    step(b)

            act.wait_ge(s_const, 48)
            act.wait_ge(cond_zero, 1)
            act.activation(cond_pad[:, :, 0:2], col("cond", 0, 16).rearrange("p (k c) -> p k c", c=2),
                           ACT.Silu).then_inc(cond_ready, 1)
            split_w(0)
            split_w(1)
            act.wait_ge(s_w3, 64)
            for stage in range(2):
                act.wait_ge(f_dve, 8 + 7 * stage)
                act.activation(fmlp[0:FILT, 2 + stage, :], fmlp[0:FILT, 0, :], ACT.Sin).then_inc(f_act, 1)
            act.activation(edecay[:], edecay[:], ACT.Exp).then_inc(f_act, 1)
            act.wait_ge(f_act, 3)
            for u in range(4):
                o, c = u // 2, u % 2
                if u > 0:
                    act.wait_ge(f_dve, 15 + 2 * u - 1)
                for dr in range(2):
                    for t in range(2):
                        w0 = o * 2048 + dr * 1024 + c * 512
                        last = act.activation(window[:, dr, t], edecay[:, w0:w0 + 512], ACT.Exp, scale=col("neg_t", t))
                last.then_inc(f_act, 1)
                act.wait_ge(f_dve, 15 + 2 * u + 1)
                if u > 0:
                    act.wait_ge(f_pe, 2 + 3 * u)
                act.activation(fsq[:], fk[:], ACT.Square).then_inc(f_act, 1)
                act.wait_ge(f_pe, 4 + 3 * u)
                act.activation(kst[:, o, :, c * 512:c * 512 + 512], ps[:, 4:8, :], ACT.Copy).then_inc(f_act, 1)
                act.wait_ge(f_pe, 5 + 3 * u)
                act.activation(rnorm[:, o, c * 4:c * 4 + 4], ps[:, 0, 0:4], ACT.Copy).then_inc(f_act, 1)
            act.wait_ge(f_act, 19)
            act.activation(rnorm[:], rnorm[:], ACT.Sqrt, bias=col("eps_filt")).then_inc(f_act, 1)

            def hidden_tiles(cols):
                return lambda b, i: hidden[:, bass.ds(2 * b + 4 * i, 2), cols]

            def ffn(f, n, cols):
                ffn_in(f, cols)
                out_proj(n, cols, hidden_tiles(cols),
                         lambda e, b: e.wait_ge(mul_done, NFI * (f + 1)))
                squares(n + 1, cols)

            squares(0, ALLC)
            affine(0, ALLC)
            ffn(0, 0, ALLC)
            affine(1, ALLC)
            split_w(G_HYIN + 1)

            def hy_in(j, i=0):
                for t in range(2):
                    tile = 2 * j + t
                    if tile == 0:
                        act.wait_ge(pad_zero, 1)
                    if t == 0:
                        act.wait_ge(w_used, G_HYIN + j + 1 + 2 * i)
                    if j > 0:
                        act.wait_ge(conv_step, 3 * (tile - 1) + 12 * i)
                    act.activation(pad[:, t, :, 1:257],
                                   ps[:, 2 * (j % 2) + t, :].rearrange("p (s n) -> p s n", s=2), ACT.Identity,
                                   bias=vec[:, bass.ds(at["hy_b_in"] + tile + 4 * i, 1)]).then_inc(pad_ready, 1)
                split_w(G_HYIN + j + 2, i)

            hy_in(0)
            hy_in(1)
            with act.Fori(0, 5) as i:
                hy_in(2, i)
                hy_in(3, i)
            for st in range(8):
                act.wait_ge(t_done, st + 1)
                if st >= 2:
                    act.wait_ge(fwd_done, st - 1)
                act.activation(zt[:, st % 2], ps[:, 6:8, :], ACT.Copy).then_inc(t_evac, 1)
                act.wait_ge(fwd_done, st + 1)
                if st >= 2:
                    act.wait_ge(inv_done, st - 1)
                act.activation(zf[:, st % 2], ps[:, 0:4, :], ACT.Copy).then_inc(fwd_evac, 1)
            out_proj(1, ALLC, lambda b, i: hyp[:, 2 * b:2 * b + 2, :],
                     lambda e, b: e.wait_ge(z_done, 8))
            squares(2, ALLC)
            affine(2, ALLC)
            split_w(G_FFN[1] + 1)
            ffn(1, 2, ALLC)
            affine(3, ALLC)
            split_w(G_FFN[2] + 1)
            ffn(2, 3, ALLC)
            act.wait_ge(comb_done, 1)
            act.activation(w_comb[:], ps[:, 7, :].rearrange("p (t a c) -> p t a c", a=2, c=16),
                           ACT.Copy).then_inc(comb_ready, 1)
            affine(4, ALLC)
            split_w(G_MLUP + 1)
            for j in range(8):
                for t in range(2):
                    tile = 2 * j + t
                    if tile == 0:
                        act.wait_ge(pad_zero, 2)
                    if t == 0:
                        act.wait_ge(w_used, G_MLUP + j + 1)
                    if j > 0:
                        act.wait_ge(qkv_done, tile - 1)
                    act.activation(pad[:, t, :, 1:257],
                                   ps[:, 2 * (j % 2) + t, :].rearrange("p (s n) -> p s n", s=2),
                                   ACT.Copy).then_inc(xm_ready, 1)
                split_w(G_MLUP + j + 2)
                for t in range(2):
                    act.wait_ge(xc_step, 3 * (2 * j + t) + 3)
                    act.activation(xc[:, t, :], xc[:, t, :], ACT.Silu).then_inc(xc_ready, 1)
                for t in range(2):
                    tile = 2 * j + t
                    act.wait_ge(kq_done, tile + 1)
                    act.activation(q_head[:, tile % HT, :], ps[:, 5, 0:LAT], ACT.Copy)
                    act.activation(k_head[:, tile % HT, :], ps[:, 4, :], ACT.Copy).then_inc(kq_evac, 1)
                    act.wait_ge(v_done, tile + 1)
                    act.activation(v_tok[:, :, tile * P:tile * P + P],
                                   ps[:, 6, :].rearrange("p (a c) -> p a c", a=4), ACT.Copy).then_inc(v_evac, 1)
                if j % 2:
                    act.wait_ge(sc_done, j // 2 + 1)
                    act.activation(score[:, j // 2], ps[:, 4:6, :], ACT.Copy, scale=DH ** -0.5).then_inc(sc_evac, 1)
            act.wait_ge(xs_done, IT)

            def z_step(j, i=0):
                act.wait_ge(w_used, G_MLUP + 9 + j + 2 * i)
                act.activation(zs[:, bass.ds(2 * j + 4 * i, 2), :], ps[:, 2 * (j % 2):2 * (j % 2) + 2, LATC],
                               ACT.Silu).then_inc(z_evac, 1)
                split_w(G_MLUP + 10 + j, i)

            z_step(0)
            z_step(1)
            act.wait_ge(row_dve, ROW["f1"])
            act.activation(row_c[R], row_f[R], ACT.Abs).then_inc(row_act, 1)
            act.wait_ge(row_act, 1)
            act.activation(row_c[R], row_c[R], ACT.Exp, scale=-1.0).then_inc(row_act, 1)
            act.wait_ge(row_act, 2)
            act.activation(row_c[R], row_c[R], ACT.Ln, bias=col("one")[R]).then_inc(row_act, 1)
            with act.Fori(0, 3) as i:
                z_step(2, i)
                z_step(3, i)
            act.wait_ge(row_dve, ROW["m"])
            act.activation(row_c[R], row_d[R], ACT.Exp, scale=-1.0).then_inc(row_act, 1)
            act.wait_ge(rcol_done, 1)
            act.activation(acols[:, 0:32], ps[:, 6, 0:32], ACT.Copy).then_inc(rcol_ready, 1)
            for it in range(8):
                for dr in range(2):
                    act.wait_ge(a_dve, A_STEPS * it + dr + 1)
                    act.activation(pd[:, dr, :], pd[:, dr, :], ACT.Exp).then_inc(a_exp, 1)
                if it > 0:
                    act.wait_ge(pv_done, it)
                    act.activation(ht[(it - 1) % 2][:, (it - 1) // 2 * DH:((it - 1) // 2 + 1) * DH], ps[:, 7, :],
                                   ACT.Copy).then_inc(pv_evac, 1)
                act.wait_ge(pt_done, it + 1)
                if it >= 2:
                    act.wait_ge(pv_done, it - 1)
                act.activation(pt[:, it % 2], ps[:, 6, :].rearrange("p (a c) -> p a c", a=4),
                               ACT.Copy).then_inc(pt_evac, 1)
            act.wait_ge(pv_done, 8)
            act.activation(ht[1][:, 3 * DH:4 * DH], ps[:, 7, :], ACT.Copy).then_inc(pv_evac, 1)
            act.wait_ge(stat_done, 16)
            act.activation(acols[:, 152:160], acols[:, 64:80].rearrange("p (a b) -> p a b", b=2)[:, :, 1],
                           ACT.Sqrt, bias=col("eps_ml")).then_inc(hn_std, 1)
            out_proj(4, LATC, lambda b, i: ym[:, bass.ds(2 * b + 4 * i, 2), :],
                     lambda e, b: e.wait_ge(ym_step, 2 * IT))
            squares(5, LATC)
            affine(5, LATC)
            split_w(G_FFN[3] + 1)
            ffn(3, 5, LATC)
            for k in range(KT):
                act.wait_ge(tn_ready, 48 + k + 1)
                act.activation(out_sb[:, k, :], tn[:, k % 2, LATC], ACT.Copy, scale=col("final_g", k)).then_inc(out_ready, 1)

        @block.vector
        def _(dve):
            def split_w(g, i=0):
                if g >= N_BLOCKS:
                    return
                dve.wait_ge(w_hi_done, g + 1 + 2 * i)
                dve.tensor_tensor(w_lo[:, g % 2, :], w_raw[:, g % 2, :], w_hi[:, g % 2, :].bitcast(F32),
                                  ALU.subtract).then_inc(w_lo_done, 1)

            def ada_copy(q):
                dve.wait_ge(ada_used, 2 * q + 2)
                if not isinstance(q, int) or q > 0:
                    dve.wait_ge(ada_cols, q)
                dve.tensor_copy(ada_part[:], ps[:, 4, :]).then_inc(ada_evac, 1)

            def ada_bias(q):
                dve.wait_ge(ada_cols, q + 1)
                b = vec[:, bass.ds(at["ada_b"] + 4 * q, 4)].rearrange("p (a b) -> p a b", b=1)
                dve.tensor_tensor(mods[:, bass.ds(4 * q, 4), :], ps[:, 5, 0:8].rearrange("p (a b) -> p a b", b=2),
                                  b.to_broadcast([P, 4, 2]), ALU.add).then_inc(ada_mods, 1)

            def coefs(n):
                dve.wait_ge(ada_mods, ADA_PAIRS * (n + 1))
                g = col("norm_g", 8 * n, 8).rearrange("p (a b) -> p a b", b=1).to_broadcast([P, KT, 2])
                dve.scalar_tensor_tensor(coef_a[:, n], mods[:, 24 * n + 8:24 * n + 16, :], 1.0, g,
                                         ALU.add, ALU.mult).then_inc(coef_ready, 1)
                dve.tensor_scalar(coef_g[:, n], mods[:, 24 * n + 16:24 * n + 24, :], 1.0 if n % 3 == 1 else 0.5,
                                  None, ALU.mult).then_inc(coef_ready, 1)

            def norm(n, cols, final=False):
                w = (cols.stop - cols.start) // P
                dve.wait_ge(std_ready, n + 1)
                dve.reciprocal(cols4[:, 1, 0:w], cols4[:, 0, 0:w]).then_inc(rstd_ready, 1)
                dve.wait_ge(rstd_ready, n + 1)
                for t in range(w):
                    last = dve.tensor_scalar(diag[:, t, :], ident[:], cols4[:, 1, t:t + 1], None, ALU.mult)
                last.then_inc(diag_ready, 1)
                dve.wait_ge(rb_ready, n + 1)

                def lo(k):
                    dve.wait_ge(uhi_ready, 8 * n + k + 1)
                    dve.tensor_tensor(act_lo[:, k, cols], uf[:, k % 2, cols], act_hi[:, k, cols].bitcast(F32),
                                      ALU.subtract).then_inc(u_ready, 1)

                for k in range(KT):
                    if k >= 2:
                        dve.wait_ge(out_ready if final else uf_ready, k - 1 + (0 if final else 8 * n))
                    dve.tensor_tensor(tn[:, k % 2, cols], h[:, k, cols], ps[:, 6, cols], ALU.mult).then_inc(tn_ready, 1)
                    if k > 0 and not final:
                        lo(k - 1)
                if not final:
                    lo(KT - 1)

            def ffn_in(f, cols, q0=0, n_ada=0, extra=None):
                g0 = G_FFN[f]

                def step(p, i=0, ada=False):
                    split_w(g0 + 2 * p + 2, i)
                    if ada:
                        ada_copy(q0 + p + i)
                    dve.wait_ge(silu_done, NFI * f + p + 1 + i)
                    dve.wait_ge(w_used, g0 + 2 * p + 2 + 2 * i)
                    dve.tensor_tensor(hidden[:, bass.ds(2 * p + 2 * i, 2), cols], silu_g[:, :, cols],
                                      ps[:, 2:4, cols], ALU.mult).then_inc(mul_done, 1)
                    split_w(g0 + 2 * p + 3, i)
                    if ada:
                        ada_bias(q0 + p + i)

                if extra is not None:
                    ada_copy(extra)
                    ada_bias(extra)
                step(0, 0, n_ada > 0)
                if n_ada > 1:
                    with dve.Fori(0, n_ada - 1) as i:
                        step(1, i, True)
                if n_ada < NFI:
                    first = max(n_ada, 1)
                    with dve.Fori(0, NFI - first) as i:
                        step(first, i)

            def out_proj(o, cols):
                g0, nb = OUT_BLOCKS[o], OUT_N[o]

                def split_in(b, src, i=0):
                    dve.wait_ge(in_hi, IN_BEFORE[o] + b + 1 + 2 * i)
                    s = 2 * (b % 2)
                    dve.tensor_tensor(act_lo[:, s:s + 2, cols], src(b, i), act_hi[:, s:s + 2, cols].bitcast(F32),
                                      ALU.subtract).then_inc(in_lo, 1)

                if o == 1:
                    src = lambda b, i: hyp[:, 2 * b:2 * b + 2, :]
                elif o == 4:
                    src = lambda b, i: ym[:, bass.ds(2 * b + 4 * i, 2), :]
                else:
                    src = lambda b, i: hidden[:, bass.ds(2 * b + 4 * i, 2), cols]

                def step(b, i=0):
                    split_w(g0 + b + 2, i)
                    if b + 2 < nb:
                        split_in(b + 2, src, i)

                split_in(0, src)
                split_in(1, src)
                if o < 5:
                    coefs(o + 1)
                loops = (nb - 3) // 2
                if loops:
                    with dve.Fori(0, loops) as i:
                        step(0, i)
                        step(1, i)
                for b in range(2 * loops, nb - 1):
                    step(b)
                dve.wait_ge(coef_ready, 2 * o + 2)
                for m in range(KT):
                    dve.wait_ge(y_done, 8 * o + m + 1)
                    for c, cd in SEQS:
                        if c.start >= cols.start:
                            last = dve.scalar_tensor_tensor(h[:, m, c], ps[:, m, c], coef_g[:, o, m, cd:cd + 1],
                                                            h[:, m, c], ALU.mult, ALU.add)
                    last.then_inc(h_ready, 1)

            dve.memset(cond_pad[:], 0.0).then_inc(cond_zero, 1)
            split_w(0)
            split_w(1)
            dve.memset(fmlp[FILT:FILT + 1, 3, :], 1.0).then_inc(f_dve, 1)
            dve.wait_ge(s_const, 48)
            two_pi = 2 * math.pi
            c1 = 6.28125
            c2 = float(np.float32(np.round((two_pi - c1) * 2 ** 22) / 2 ** 22))
            c3 = float(np.float32(two_pi - c1 - c2))
            pi32 = float(np.nextafter(np.float32(math.pi), np.float32(0)))
            magic = 1.5 * 2 ** 23
            X, N = fmlp[0:FILT, 0, :], fmlp[0:FILT, 1, :]
            for stage in range(2):
                n = 1 + 7 * stage
                dve.wait_ge(f_pe, stage + 1)
                bias = col("f_b1" if stage == 0 else "f_b2")[0:FILT]
                dve.tensor_scalar(X, ps[0:FILT, 2, 0:256], bias, col("f_freq", stage)[0:FILT],
                                  ALU.add, ALU.mult).then_inc(f_dve, 1)
                dve.wait_ge(f_dve, n + 1)
                dve.tensor_scalar(N, X, 1.0 / two_pi, magic, ALU.mult, ALU.add).then_inc(f_dve, 1)
                dve.wait_ge(f_dve, n + 2)
                dve.tensor_scalar(N, N, magic, None, ALU.subtract).then_inc(f_dve, 1)
                dve.wait_ge(f_dve, n + 3)
                dve.scalar_tensor_tensor(X, N, -c1, X, ALU.mult, ALU.add).then_inc(f_dve, 1)
                dve.wait_ge(f_dve, n + 4)
                dve.scalar_tensor_tensor(X, N, -c2, X, ALU.mult, ALU.add).then_inc(f_dve, 1)
                dve.wait_ge(f_dve, n + 5)
                dve.scalar_tensor_tensor(X, N, -c3, X, ALU.mult, ALU.add).then_inc(f_dve, 1)
                dve.wait_ge(f_dve, n + 6)
                dve.tensor_scalar(X, X, pi32, -pi32, ALU.min, ALU.max).then_inc(f_dve, 1)
            for u in range(4):
                dve.wait_ge(f_pe, 3 + 3 * u)
                dve.wait_ge(f_act, 4 + 4 * u)
                if u > 0:
                    dve.wait_ge(f_act, 1 + 4 * u)
                for t in range(2):
                    dve.tensor_tensor(fk[:, 0, t], ps[:, 2 * t, :], window[:, 0, t], ALU.mult)
                    last = dve.scalar_tensor_tensor(fk[:, 1, t], ps[:, 2 * t + 1, :], col("tap_mask", t),
                                                    window[:, 1, t], ALU.mult, ALU.mult)
                last.then_inc(f_dve, 1)
                dve.wait_ge(f_dve, 15 + 2 * u + 1)
                if u > 0:
                    dve.wait_ge(f_pe, 1 + 3 * u)
                dve.tensor_tensor(fsd[:, 0], fk[:, 0], fk[:, 1], ALU.add)
                dve.tensor_tensor(fsd[:, 1], fk[:, 0], fk[:, 1], ALU.subtract).then_inc(f_dve, 1)
            dve.wait_ge(f_act, 20)
            dve.reciprocal(rnorm[:], rnorm[:]).then_inc(f_dve, 1)
            dve.wait_ge(s_tok, 16)
            dve.wait_ge(s_pos, 16)
            for m in range(KT):
                dve.tensor_tensor(h[:, m, LATC], h[:, m, LATC], pos[:, m, :], ALU.add).then_inc(h_ready, 1)
            ada_copy(0)
            ada_bias(0)
            with dve.Fori(1, 7) as q:
                ada_copy(q)
                ada_bias(q)
            coefs(0)
            norm(0, ALLC)
            ffn_in(0, ALLC, q0=7, n_ada=NFI)
            out_proj(0, ALLC)
            norm(1, ALLC)
            split_w(G_HYIN + 1)
            dve.memset(pad[:], 0.0).then_inc(pad_zero, 1)

            def conv(dst, t, w0, wn, b0, tile, i, per, step_sem):
                def c(first):
                    return vec[:, bass.ds(first + tile + per * i, 1)]

                n = 3 * tile + 3 * per * i
                dve.tensor_scalar(dst, pad[:, t, :, 1:257], c(w0 + wn), c(b0), ALU.mult, ALU.add).then_inc(step_sem, 1)
                dve.wait_ge(step_sem, n + 1)
                dve.scalar_tensor_tensor(dst, pad[:, t, :, 0:256], c(w0), dst, ALU.mult, ALU.add).then_inc(step_sem, 1)
                dve.wait_ge(step_sem, n + 2)
                dve.scalar_tensor_tensor(dst, pad[:, t, :, 2:258], c(w0 + 2 * wn), dst,
                                         ALU.mult, ALU.add).then_inc(step_sem, 1)

            def hy_in(j, i=0):
                for t in range(2):
                    tile = 2 * j + t
                    dve.wait_ge(pad_ready, tile + 1 + 4 * i)
                    dst = hyp[:, bass.ds(tile + 4 * i, 1), :].rearrange("p a (s n) -> p (a s) n", s=2)
                    conv(dst, t, at["hy_conv_w"], 24, at["hy_conv_b"], tile, i, 4, conv_step)
                split_w(G_HYIN + j + 2, i)

            hy_in(0)
            hy_in(1)
            with dve.Fori(0, 5) as i:
                hy_in(2, i)
                hy_in(3, i)
            dve.wait_ge(conv_step, 72)
            steps = [0]

            def own(ins):
                steps[0] += 1
                ins.then_inc(hy_step, 1)

            def pointwise(st):
                o, c = st // 4, st % 2
                z, k = zf[:, st % 2], kst[:, o, :, c * 512:c * 512 + 512]
                zr, zi, kr, ki = z[:, 0:2], z[:, 2:4], k[:, 0:2], k[:, 2:4]
                if st > 0:
                    dve.wait_ge(pw_done, st)
                if st > 1:
                    dve.wait_ge(z_done, st - 1)
                dve.wait_ge(fwd_evac, st + 1)
                dve.tensor_tensor(pwa[:], zi, ki, ALU.mult)
                own(dve.tensor_tensor(pwb[:], zr, ki, ALU.mult))
                dve.wait_ge(hy_step, steps[0])
                own(dve.tensor_tensor(zr, zr, kr, ALU.mult))
                own(dve.tensor_tensor(zi, zi, kr, ALU.mult))
                dve.wait_ge(hy_step, steps[0] - 1)
                dve.tensor_tensor(zr, zr, pwa[:], ALU.subtract)
                dve.wait_ge(hy_step, steps[0])
                dve.tensor_tensor(zi, zi, pwb[:], ALU.add).then_inc(pw_done, 1)

            def gate(st):
                o, s, c = st // 4, st // 2 % 2, st % 2
                v = hyp[:, 4 * c:4 * c + 4, s * 256:s * 256 + 256]
                x = hyp[:, 8 + 8 * o + 4 * c:12 + 8 * o + 4 * c, s * 256:s * 256 + 256]
                dve.wait_ge(pw_done, min(st + 2, 8))
                if st > 0:
                    dve.wait_ge(z_done, st)
                for ct in range(4):
                    ins = dve.tensor_scalar(gate_t[:, ct], v[:, ct], col("hy_skip", 8 * o + 4 * c + ct), None, ALU.mult)
                own(ins)
                dve.wait_ge(inv_done, st + 1)
                dve.wait_ge(hy_step, steps[0])
                for ct in range(4):
                    ins = dve.scalar_tensor_tensor(gate_t[:, ct], ps[:, 4 + ct // 2, ct % 2 * 256:ct % 2 * 256 + 256],
                                                   rnorm[:, o, 4 * c + ct:4 * c + ct + 1], gate_t[:, ct],
                                                   ALU.mult, ALU.add)
                own(ins)
                dve.wait_ge(hy_step, steps[0])
                dve.tensor_tensor(v, gate_t[:], x, ALU.mult).then_inc(z_done, 1)

            for st in range(9):
                if st < 8:
                    pointwise(st)
                if st > 0:
                    gate(st - 1)
            dve.wait_ge(z_done, 8)
            dve.wait_ge(coef_ready, 4)
            b = col("hy_b_out", 0, 8).rearrange("p (a b) -> p a b", b=1).to_broadcast([P, KT, 2])
            own(dve.tensor_tensor(pwa[:, 0, 0:16].rearrange("p (a b) -> p a b", b=2), coef_g[:, 1], b, ALU.mult))
            dve.wait_ge(hy_step, steps[0])
            for m in range(KT):
                for c, cd in SEQS:
                    ins = dve.tensor_scalar(h[:, m, c], h[:, m, c], pwa[:, 0, 2 * m + cd:2 * m + cd + 1], None, ALU.add)
            own(ins)
            dve.wait_ge(hy_step, steps[0])
            out_proj(1, ALLC)
            norm(2, ALLC)
            split_w(G_FFN[1] + 1)
            ffn_in(1, ALLC, q0=19, n_ada=NFI, extra=18)
            out_proj(2, ALLC)
            norm(3, ALLC)
            split_w(G_FFN[2] + 1)
            ffn_in(2, ALLC, q0=30, n_ada=6)
            out_proj(3, ALLC)
            norm(4, ALLC)
            split_w(G_MLUP + 1)
            dve.memset(pad[:], 0.0).then_inc(pad_zero, 1)
            for j in range(8):
                for t in range(2):
                    tile = 2 * j + t
                    dve.wait_ge(xm_ready, tile + 1)
                    if j > 0:
                        dve.wait_ge(qkv_done, tile - 1)
                        dve.wait_ge(xs_done, tile - 1)
                    dst = xc[:, t, :].rearrange("p (s n) -> p s n", s=2)
                    conv(dst, t, at["ml_conv_w"], 16, at["ml_conv_b"], tile, 0, 0, xc_step)
                split_w(G_MLUP + j + 2)
                for t in range(2):
                    tile = 2 * j + t
                    dve.wait_ge(xc_ready, tile + 1)
                    dve.tensor_scalar(xs[:, tile, :], xc[:, t, LATC], col("ml_skip", tile), None,
                                      ALU.mult).then_inc(xs_done, 1)
            split_w(G_MLUP + 10)
            split_w(G_MLUP + 11)
            dve.wait_ge(qkv_done, IT)
            dve.memset(cond_pad[:], 0.0).then_inc(row_dve, 1)
            zeros = cond_pad[R].rearrange("p k c -> p (k c)")
            for g in range(2):
                dve.tensor_copy(gsum[32 * g:32 * g + 16, :], ps[32 * g:32 * g + 16, 7, :]).then_inc(row_dve, 1)
            dve.wait_ge(sel_done, 2)
            for dr in range(2):
                dve.tensor_scalar(row_i[R, dr], ps[R, 4 + 2 * dr, :], col("b_gate", 2 * dr)[R], None,
                                  ALU.add).then_inc(row_dve, 1)
                dve.tensor_scalar(row_f[R, dr], ps[R, 5 + 2 * dr, :], col("b_gate", 2 * dr + 1)[R], None,
                                  ALU.add).then_inc(row_dve, 1)
            dve.wait_ge(row_act, 3)
            dve.scalar_tensor_tensor(row_f[R], row_f[R], 0.0, row_c[R], ALU.min, ALU.subtract).then_inc(row_dve, 1)

            def scans(out, src, second, op, steps_of):
                dve.wait_ge(row_dve, ROW[steps_of[0]] - 1)
                for dr in range(2):
                    for part, c in enumerate((slice(0, CTX), slice(CTX, TOK))):
                        def view(x):
                            return x[:, ::-1] if dr else x
                        if part == 0:
                            init = 0.0
                        else:
                            init = out[R, dr, CTX - 1:CTX] if dr == 0 else out[R, dr, 0:1]
                            dve.wait_ge(row_dve, ROW[steps_of[2 * dr]])
                        s = view(src[R, dr, c])
                        dve.tensor_tensor_scan(view(out[R, dr, c]), s, zeros if second is None else s, init,
                                               op, op).then_inc(row_dve, 1)

            scans(row_d, row_f, None, ALU.add, ("cum0", "cum1", "cum2", "cum3"))
            dve.wait_ge(row_dve, ROW["cum3"])
            dve.tensor_tensor(row_g[R], row_i[R], row_d[R], ALU.subtract).then_inc(row_dve, 1)
            scans(row_e, row_g, True, ALU.max, ("max0", "max1", "max2", "max3"))
            dve.wait_ge(row_dve, ROW["max3"])
            dve.tensor_tensor(row_d[R], row_d[R], row_e[R], ALU.add).then_inc(row_dve, 1)
            with dve.Fori(0, 3) as i:
                split_w(G_MLUP + 12, i)
                split_w(G_MLUP + 13, i)
            dve.wait_ge(s_mask, 16)
            dve.wait_ge(rcol_ready, 1)
            dve.wait_ge(sc_evac, HEADS)
            rc = acols[:, 0:32].rearrange("p (q d j e) -> p q d j e", q=2, d=2, j=2)

            def stats(it):
                dve.wait_ge(pv_evac, it + 1)
                hv = ht[it % 2][:, it // 2 * DH:(it // 2 + 1) * DH]
                dve.bn_stats(acols[:, 104 + 6 * it:110 + 6 * it], hv).then_inc(stat_done, 1)
                dve.wait_ge(stat_done, 2 * it + 1)
                dve.bn_aggr(acols[:, 64 + 2 * it:66 + 2 * it], acols[:, 104 + 6 * it:110 + 6 * it]).then_inc(stat_done, 1)

            for it in range(8):
                hd, jt = it // 2, it % 2
                n = A_STEPS * it
                qn = acols[:, 32 + 2 * it:34 + 2 * it]
                rd = acols[:, 48 + 2 * it:50 + 2 * it]
                dve.wait_ge(bc_done, hd + 1)
                if it > 0:
                    dve.wait_ge(a_dve, n)
                for dr in range(2):
                    dve.tensor_scalar(pd[:, dr, :], ps[:, 4 + dr, :], rc[:, 0, dr, jt, hd:hd + 1], 0.0,
                                      ALU.subtract, ALU.min).then_inc(a_dve, 1)
                for dr in range(2):
                    dve.wait_ge(a_exp, 2 * it + dr + 1)
                    dve.tensor_tensor(pd[:, dr, LATC], pd[:, dr, LATC], mask[:, dr, jt, :], ALU.mult).then_inc(a_dve, 1)
                    dve.wait_ge(a_dve, n + 3 + 2 * dr)
                    dve.scalar_tensor_tensor(pd[:, dr, :], pd[:, dr, :], 1.0, score[:, hd, jt, :], ALU.mult, ALU.mult,
                                             accum_out=qn[:, dr:dr + 1]).then_inc(a_dve, 1)
                dve.wait_ge(a_dve, n + 6)
                dve.scalar_tensor_tensor(rd, qn, -1.0, qn, ALU.mult, ALU.max).then_inc(a_dve, 1)
                dve.wait_ge(a_dve, n + 7)
                dve.tensor_tensor(rd, rd, rc[:, 1, :, jt, hd], ALU.max).then_inc(a_dve, 1)
                dve.wait_ge(a_dve, n + 8)
                dve.reciprocal(rd, rd).then_inc(a_dve, 1)
                dve.wait_ge(a_dve, n + 9)
                if it > 0:
                    dve.wait_ge(pt_done, it)
                dve.tensor_scalar(pc[:], pd[:, 0, :], rd[:, 0:1], None, ALU.mult).then_inc(a_dve, 1)
                dve.wait_ge(a_dve, n + 10)
                dve.scalar_tensor_tensor(pc[:], pd[:, 1, :], rd[:, 1:2], pc[:], ALU.mult, ALU.add).then_inc(a_dve, 1)
                if it > 0:
                    stats(it - 1)
            stats(7)
            dve.wait_ge(hn_std, 1)
            dve.reciprocal(acols[:, 160:168], acols[:, 152:160]).then_inc(hn_ready, 1)
            dve.wait_ge(hn_ready, 1)
            dve.wait_ge(pv_evac, 8)
            for it in range(8):
                hv = ht[it % 2][:, it // 2 * DH:(it // 2 + 1) * DH]
                dve.tensor_scalar(hv, hv, acols[:, 64 + 2 * it:65 + 2 * it], acols[:, 160 + it:161 + it],
                                  ALU.subtract, ALU.mult).then_inc(hn_ready, 1)
            dve.wait_ge(z_evac, 8)
            for ct in range(IT):
                dve.wait_ge(hnt_done, ct + 1)
                dve.scalar_tensor_tensor(ym[:, ct, :], ps[:, 6 + ct % 2, 0:256], col("ml_norm_g", ct), xs[:, ct, :],
                                         ALU.mult, ALU.add).then_inc(ym_step, 1)
                dve.wait_ge(ym_step, 2 * ct + 1)
                dve.tensor_tensor(ym[:, ct, :], ym[:, ct, :], zs[:, ct, :], ALU.mult).then_inc(ym_step, 1)
            out_proj(4, LATC)
            norm(5, LATC)
            split_w(G_FFN[3] + 1)
            ffn_in(3, LATC)
            out_proj(5, LATC)
            norm(6, LATC, final=True)

        @block.tensor
        def _(pe):
            def product(out, w, x, slot_w, start, stop):
                (wh, wl), (xh, xl) = w, x
                pe.matmul(out, wh, xh, start=start, stop=False)
                pe.matmul(out, wh, xl, start=False, stop=False)
                return pe.matmul(out, wl, xh, start=False, stop=stop)

            def in_block(g, i, bank, cols, norm_n=None):
                pe.wait_ge(w_lo_done, g + 1 + 2 * i)
                s = g % 2
                wh = w_hi[:, s, :].rearrange("p (k c) -> p k c", c=256)
                wl = w_lo[:, s, :].rearrange("p (k c) -> p k c", c=256)
                for k in range(KT):
                    if norm_n is not None:
                        pe.wait_ge(u_ready, 8 * norm_n + k + 1)
                    for t in range(2):
                        c = slice(t * P, t * P + P)
                        mm = product(ps[:, bank + t, cols], (wh[:, k, c], wl[:, k, c]),
                                     (act_hi[:, k, cols], act_lo[:, k, cols]), s, k == 0, k == KT - 1)
                mm.then_inc(w_used, 1)

            def ada_pair(q):
                if not isinstance(q, int) or q > 0:
                    pe.wait_ge(ada_evac, q)
                for s in range(2):
                    pe.wait_ge(ada_loaded[s], 16 * q + 16)
                    for k in range(KT):
                        g = 32 * (k % 4)
                        mm = pe.matmul(ps[g:g + 32, 4, s * 256:s * 256 + 256], cond_pad[:, k, :], ada_raw[:, s, k, :],
                                       start=k < 4, stop=k >= 4)
                    mm.then_inc(ada_used, 1)

            def ada_turn(q):
                pe.wait_ge(ada_evac, q + 1)
                if not isinstance(q, int) or q > 0:
                    pe.wait_ge(ada_mods, q)
                for t in range(4):
                    mm = pe.matmul(ps[:, 5, 2 * t:2 * t + 2], ada_part[:, t * P:t * P + P], col("cond_sel", 0, 2),
                                   start=True, stop=True)
                mm.then_inc(ada_cols, 1)

            def square_sum(n, m, cols, block_done=False):
                pe.wait_ge(sq_ready, 8 * n + m + 1)
                w = (cols.stop - cols.start) // P
                for t in range(w):
                    c = slice(cols.start + t * P, cols.start + t * P + P)
                    mm = pe.matmul(ps[:, 0, t:t + 1], sq[:, m % 2, c], col("mean_w"), start=m == 0 and t == 0,
                                   stop=m == KT - 1, skip_group_check=True)
                    if t == 0 and block_done:
                        mm.then_inc(w_used, 1)
                mm.then_inc(ss_done, 1)

            def rms_rows(n, cols):
                pe.wait_ge(diag_ready, n + 1)
                w = (cols.stop - cols.start) // P
                pe.matmul(ps[:, 6, cols], ones[:], diag[:, 0:w, :], start=True, stop=True).then_inc(rb_ready, 1)

            def ffn_in(f, n, cols, q0=0, n_ada=0, extra=None):
                g0 = G_FFN[f]

                def step(p, i=0, ada=False):
                    if p > 0:
                        pe.wait_ge(silu_done, NFI * f + p + i)
                    in_block(g0 + 2 * p, i, 0, cols, n if p == 0 else None)
                    if ada:
                        ada_pair(q0 + p + i)
                    if p > 0:
                        pe.wait_ge(mul_done, NFI * f + p + i)
                    in_block(g0 + 2 * p + 1, i, 2, cols)
                    if ada:
                        ada_turn(q0 + p + i)

                if extra is not None:
                    ada_pair(extra)
                    ada_turn(extra)
                step(0, 0, n_ada > 0)
                if n_ada > 1:
                    with pe.Fori(0, n_ada - 1) as i:
                        step(1, i, True)
                if n_ada < NFI:
                    first = max(n_ada, 1)
                    with pe.Fori(0, NFI - first) as i:
                        step(first, i)

            def out_proj(o, cols, pairs):
                g0, nb = OUT_BLOCKS[o], OUT_N[o]
                n = o + 1
                if pairs:
                    pe.wait_ge(ada_mods, pairs)

                def operands(b):
                    s, sw = b % 2, (g0 + b) % 2
                    wh = w_hi[:, sw, :].rearrange("p (k c) -> p k c", c=D)
                    wl = w_lo[:, sw, :].rearrange("p (k c) -> p k c", c=D)
                    return lambda k, m: ((wh[:, k, m * P:m * P + P], wl[:, k, m * P:m * P + P]),
                                         (act_hi[:, 2 * s + k, cols], act_lo[:, 2 * s + k, cols]))

                def step(b, i=0):
                    pe.wait_ge(w_lo_done, g0 + b + 1 + 2 * i)
                    pe.wait_ge(in_lo, IN_BEFORE[o] + b + 1 + 2 * i)
                    ops = operands(b)
                    for k in range(2):
                        for m in range(KT):
                            w, x = ops(k, m)
                            mm = product(ps[:, m, cols], w, x, 0, b == 0 and k == 0, False)
                    mm.then_inc(w_used, 1)

                step(0)
                loops = (nb - 3) // 2
                if loops:
                    with pe.Fori(0, loops) as i:
                        step(1, i)
                        step(2, i)
                for b in range(1 + 2 * loops, nb - 1):
                    step(b)
                b = nb - 1
                pe.wait_ge(w_lo_done, g0 + b + 1)
                pe.wait_ge(in_lo, IN_BEFORE[o] + b + 1)
                ops = operands(b)
                for m in range(KT):
                    for k in range(2):
                        w, x = ops(k, m)
                        mm = product(ps[:, m, cols], w, x, 0, False, k == 1)
                    mm.then_inc(y_done, 1)
                    if m >= 2:
                        square_sum(n, m - 2, cols)
                square_sum(n, 6, cols, block_done=True)
                square_sum(n, 7, cols)

            pe.wait_ge(s_w3, 64)
            pe.matmul(ps[0:FILT, 2, 0:256], fsmall[0:EMB, 0:FILT], fsmall[0:EMB, FILT:FILT + 256],
                      start=True, stop=True).then_inc(f_pe, 1)
            pe.wait_ge(f_act, 1)
            pe.matmul(ps[0:FILT, 2, 0:256], fsmall[0:FILT, FILT + 256:FILT + 320], fmlp[0:FILT, 2, :],
                      start=True, stop=True).then_inc(f_pe, 1)
            pe.wait_ge(f_act, 2)
            for u in range(4):
                o, c = u // 2, u % 2
                if u > 0:
                    pe.wait_ge(f_act, 3 + 4 * u)
                for t in range(2):
                    for dr in range(2):
                        w0 = o * 2048 + dr * 1024 + c * 512
                        mm = pe.matmul(ps[:, 2 * t + dr, :], fmlp[0:FILT + 1, 3, t * P:t * P + P],
                                       w3aug[0:FILT + 1, w0:w0 + 512], start=True, stop=True)
                mm.then_inc(f_pe, 1)
                pe.wait_ge(f_dve, 15 + 2 * u + 2)
                for part in range(2):
                    for m in range(2):
                        for t in range(2):
                            mm = pe.matmul(ps[:, 4 + 2 * part + m, :], dft_f[:, part, t, m * P:m * P + P],
                                           fsd[:, part, t], start=t == 0, stop=t == 1)
                mm.then_inc(f_pe, 1)
                pe.wait_ge(f_act, 5 + 4 * u)
                for ct in range(4):
                    for q in range(4):
                        mm = pe.matmul(ps[:, 0, ct:ct + 1], fsq[:, q // 2, q % 2, ct * P:ct * P + P], ones[:, 0:1],
                                       start=q == 0, stop=q == 3)
                mm.then_inc(f_pe, 1)
            pe.wait_ge(cond_ready, 1)
            pe.wait_ge(s_const, 48)
            pe.wait_ge(f_act, 19)
            ada_pair(0)
            ada_turn(0)
            with pe.Fori(1, 7) as q:
                ada_pair(q)
                ada_turn(q)
            for m in range(KT):
                square_sum(0, m, ALLC)
            rms_rows(0, ALLC)
            ffn_in(0, 0, ALLC, q0=7, n_ada=NFI)
            out_proj(0, ALLC, 18)
            rms_rows(1, ALLC)

            def hy_in(j, i=0):
                if j >= 2:
                    pe.wait_ge(pad_ready, 2 * j - 2 + 4 * i)
                in_block(G_HYIN + j, i, 2 * (j % 2), ALLC, 1 if j == 0 else None)

            hy_in(0)
            hy_in(1)
            with pe.Fori(0, 5) as i:
                hy_in(2, i)
                hy_in(3, i)

            def turn(st):
                o, s, c = st // 4, st // 2 % 2, st % 2
                if o == 0:
                    pe.wait_ge(conv_step, 24 if st else 72)
                else:
                    pe.wait_ge(z_done, st - 3)
                if st > 0:
                    pe.wait_ge(t_evac, st)
                else:
                    pe.wait_ge(rb_ready, 2)
                for t in range(2):
                    for ct in range(4):
                        n0 = s * 256 + t * P
                        mm = pe.transpose(ps[:, 6 + t, ct * P:ct * P + P], hyp[:, 4 * c + ct, n0:n0 + P], ident[:])
                mm.then_inc(t_done, 1)

            def forward(st):
                pe.wait_ge(t_evac, st + 1)
                if st > 0:
                    pe.wait_ge(fwd_evac, st)
                else:
                    pe.wait_ge(s_dft, 32)
                for part in range(2):
                    for m in range(2):
                        for t in range(2):
                            mm = pe.matmul(ps[:, 2 * part + m, :], dft_h[:, part, t, m * P:m * P + P],
                                           zt[:, st % 2, t, :], start=t == 0, stop=t == 1)
                mm.then_inc(fwd_done, 1)

            def inverse(st):
                pe.wait_ge(pw_done, st + 1)
                if st > 0:
                    pe.wait_ge(z_done, st)
                for ct in range(4):
                    for q in range(4):
                        mm = pe.matmul(ps[:, 4 + ct // 2, ct % 2 * 256:ct % 2 * 256 + 256],
                                       zf[:, st % 2, q, ct * P:ct * P + P], dft_i[:, q // 2, q % 2, :],
                                       start=q == 0, stop=q == 3)
                mm.then_inc(inv_done, 1)

            for st in range(9):
                if st < 8:
                    turn(st)
                    forward(st)
                if st > 0:
                    inverse(st - 1)
            out_proj(1, ALLC, 0)
            rms_rows(2, ALLC)
            ffn_in(1, 2, ALLC, q0=19, n_ada=NFI, extra=18)
            out_proj(2, ALLC, 30)
            rms_rows(3, ALLC)
            ffn_in(2, 3, ALLC, q0=30, n_ada=6)
            out_proj(3, ALLC, 36)
            pe.wait_ge(s_bdt, 32)
            for t in range(IT):
                o0 = 32 * t
                pe.matmul(ps[:, 7, o0:o0 + 16], bdt[:, 0, t, :], wg[:, 0, t, :], start=True, stop=False)
                pe.matmul(ps[:, 7, o0:o0 + 16], bdt[:, 1, t, :], wg[:, 1, t, :], start=False, stop=True)
                mm = pe.matmul(ps[:, 7, o0 + 16:o0 + 32], bdt[:, 2, t, :], wg[:, 2, t, :], start=True, stop=True)
            mm.then_inc(comb_done, 1)
            rms_rows(4, ALLC)

            def up(j):
                if 2 <= j <= 9:
                    pe.wait_ge(xm_ready, 2 * j - 2)
                in_block(G_MLUP + j, 0, 2 * (j % 2), ALLC if j < 8 else LATC, 4 if j == 0 else None)

            def qkv(j):
                for t in range(2):
                    tile = 2 * j + t
                    hd, ht_i = tile // HT, tile % HT
                    b = bd[:, hd % 2, ht_i]
                    if ht_i == 0:
                        pe.wait_ge(bd_loaded[hd % 2], 16 * (hd // 2 + 1))
                        if hd > 0:
                            pe.wait_ge(sc_evac, hd)
                    pe.wait_ge(xc_ready, tile + 1)
                    if tile > 0:
                        pe.wait_ge(kq_evac, tile)
                    pe.matmul(ps[:, 5, 0:LAT], b[:, 0], xc[:, t, LATC], start=True, stop=True)
                    pe.matmul(ps[:, 4, :], b[:, 1], xc[:, t, :], start=True, stop=True).then_inc(kq_done, 1)
                    if tile > 0:
                        pe.wait_ge(v_evac, tile)
                    for s in range(4):
                        n0 = 1 + (s % 2) * P
                        mm = pe.matmul(ps[:, 6, s * P:s * P + P], pad[:, t, s // 2, n0:n0 + P], b[:, 2],
                                       start=True, stop=True)
                    mm.then_inc(v_done, 1)
                    if tile == 0:
                        pe.wait_ge(comb_ready, 1)
                    pe.matmul(ps[0:16, 7, :], w_comb[:, tile, 0, :], xc[:, t, :], start=tile == 0, stop=tile == IT - 1,
                              skip_group_check=True)
                    pe.matmul(ps[32:48, 7, :], w_comb[:, tile, 1, :], pad[:, t, :, 1:257], start=tile == 0,
                              stop=tile == IT - 1, skip_group_check=True).then_inc(qkv_done, 1)

            up(0)
            for j in range(8):
                up(j + 1)
                qkv(j)
                if j % 2:
                    hd = j // 2
                    pe.wait_ge(kq_evac, HT * (hd + 1))
                    for jt in range(2):
                        for k in range(HT):
                            mm = pe.matmul(ps[:, 4 + jt, :], q_head[:, k, jt * P:jt * P + P], k_head[:, k, :],
                                           start=k == 0, stop=k == HT - 1)
                    mm.then_inc(sc_done, 1)
            up(9)
            pe.wait_ge(row_dve, ROW["gsum1"])
            pe.wait_ge(sc_evac, HEADS)
            pe.wait_ge(v_evac, IT)
            for g in range(2):
                if g == 1:
                    pe.wait_ge(sel_done, 1)
                for r in range(4):
                    a = slice(32 * g, 32 * g + 16)
                    mm = pe.matmul(ps[R, 4 + r, :], ident[a, 32 * g + 4 * r:32 * g + 4 * r + 4], gsum[a, :],
                                   start=g == 0, stop=g == 1)
                mm.then_inc(sel_done, 1)

            def z_block(j, i):
                pe.wait_ge(z_evac, j - 1 + 2 * i)
                in_block(G_MLUP + 8 + j, i, 2 * (j % 2), LATC)

            with pe.Fori(0, 3) as i:
                z_block(2, i)
                z_block(3, i)
            pe.wait_ge(row_act, 4)
            for q, rows in enumerate((row_e, row_c)):
                for dr in range(2):
                    for jt in range(2):
                        o0 = ((q * 2 + dr) * 2 + jt) * HEADS
                        mm = pe.transpose(ps[:, 6, o0:o0 + HEADS], rows[R, dr, CTX + jt * P:CTX + jt * P + P],
                                          ident[R, 0:HEADS])
            mm.then_inc(rcol_done, 1)
            for it in range(8):
                hd, jt = it // 2, it % 2
                if jt == 0:
                    if hd > 0:
                        pe.wait_ge(a_dve, A_STEPS * (it - 1) + 2)
                    for dr in range(2):
                        mm = pe.matmul(ps[:, 4 + dr, :], ident[R, hd:hd + 1].to_broadcast([HEADS, P]), row_g[R, dr, :],
                                       start=True, stop=True)
                    mm.then_inc(bc_done, 1)
                pe.wait_ge(a_dve, A_STEPS * (it + 1))
                if it > 0:
                    pe.wait_ge(pt_evac, it)
                else:
                    pe.wait_ge(rcol_ready, 1)
                for s in range(4):
                    mm = pe.transpose(ps[:, 6, s * P:s * P + P], pc[:, s * P:s * P + P], ident[:])
                mm.then_inc(pt_done, 1)
                pe.wait_ge(pt_evac, it + 1)
                if it > 0:
                    pe.wait_ge(pv_evac, it)
                for s in range(4):
                    mm = pe.matmul(ps[:, 7, :], pt[:, it % 2, s, :], v_tok[:, s, hd * DH:(hd + 1) * DH],
                                   start=s == 0, stop=s == 3)
                mm.then_inc(pv_done, 1)
            for ct in range(IT):
                pe.wait_ge(hn_ready, 3 + 2 * (ct // HT))
                if ct >= 2:
                    pe.wait_ge(ym_step, 2 * (ct - 2) + 1)
                for jt in range(2):
                    mm = pe.transpose(ps[:, 6 + ct % 2, jt * P:jt * P + P], ht[jt][:, ct * P:ct * P + P], ident[:])
                mm.then_inc(hnt_done, 1)
            out_proj(4, LATC, 0)
            rms_rows(5, LATC)
            ffn_in(3, 5, LATC)
            out_proj(5, LATC, 0)
            rms_rows(6, LATC)


def constants():
    f = np.float32
    n = CTX
    t = np.arange(n, dtype=f)
    t_norm = (t / f(n - 1)).astype(f)
    bands = np.linspace(1e-4, BANDS - 1, BANDS, dtype=f)
    ang = ((f(2.0 * math.pi / n) * t)[:, None] * bands[None, :]).astype(f)
    feats = np.concatenate([t_norm[:, None], np.cos(ang), -np.sin(ang)], axis=-1).astype(f)
    theta = np.pi * (2 * np.arange(n)[None, :] + 1) * np.arange(n)[:, None] / (2 * n)
    fwd = np.stack([np.cos(theta), -np.sin(theta)]).reshape(2, 2, P, n).transpose(2, 0, 1, 3)
    inv = (np.stack([np.cos(theta.T), -np.sin(theta.T)]) / n).reshape(2, 2, P, n).transpose(2, 0, 1, 3)
    quarter = D // 4
    omega = (1.0 / (f(10000.0) ** (np.arange(quarter, dtype=f) / f(quarter)))).astype(f)
    rows = LAT // 64
    ang_r, ang_c = np.arange(rows, dtype=f)[:, None] * omega, np.arange(64, dtype=f)[:, None] * omega
    row_emb = np.concatenate([np.sin(ang_r), np.cos(ang_r)], axis=-1)
    col_emb = np.concatenate([np.sin(ang_c), np.cos(ang_c)], axis=-1)
    emb = np.concatenate([np.broadcast_to(row_emb[:, None, :], (rows, 64, D // 2)),
                          np.broadcast_to(col_emb[None, :, :], (rows, 64, D // 2))], axis=-1).reshape(LAT, D)
    j, s = np.arange(LAT)[:, None], np.arange(LAT)[None, :]
    mask = np.stack([s <= j, s >= j]).astype(f).reshape(2, 2, P, LAT).transpose(2, 0, 1, 3)
    return {"t_norm": t_norm, "feats": feats, "dft_f": fwd.astype(f), "dft_i": inv.astype(f),
            "pos": emb.astype(f).T.reshape(KT, P, LAT).transpose(1, 0, 2), "mask": mask}


def lay_out(x, c, ctx, c_ctx, ada_w, ada_b, norm_g, final_g, ffn_w_in, ffn_w_out, hy_w_in, hy_b_in, hy_conv_w,
            hy_conv_b, hy_f_w1, hy_f_b1, hy_f_w2, hy_f_b2, hy_f_w3, hy_f_b3, hy_f_freq, hy_log_decay, hy_skip,
            hy_w_out, hy_b_out, ml_w_up, ml_conv_w, ml_conv_b, ml_w_q, ml_w_k, ml_w_v, ml_w_gate, ml_b_gate,
            ml_norm_g, ml_skip, ml_w_down):
    f = np.float32
    const = constants()
    at, n_vec = column_places()

    def in_blocks(w):
        return w.reshape(KT, P, -1, 256).transpose(2, 1, 0, 3).reshape(-1, P, BLK)

    def out_blocks(w):
        return w.reshape(-1, 2, P, D).transpose(0, 2, 1, 3).reshape(-1, P, BLK)

    def ffn_blocks(layer, half):
        w = in_blocks(ffn_w_in[layer, half])
        pairs = np.stack([w[:NFI], w[NFI:]], axis=1).reshape(2 * NFI, P, BLK)
        return [pairs, out_blocks(ffn_w_out[layer, half])]

    hy_order = [2, 0, 1]
    hy_in = in_blocks(hy_w_in[0]).reshape(3, 4, P, BLK)[hy_order].reshape(12, P, BLK)
    w_stream = np.concatenate(ffn_blocks(0, 0) + [hy_in, out_blocks(hy_w_out[0])] + ffn_blocks(0, 1)
                              + ffn_blocks(1, 0) + [in_blocks(ml_w_up[0]), out_blocks(ml_w_down[0])]
                              + ffn_blocks(1, 1))
    assert w_stream.shape[0] == N_BLOCKS
    ada_stream = np.concatenate([in_blocks(ada_w[i]) for i in range(2)]).reshape(-1, P, KT, 256)

    vec = np.zeros((P, n_vec), f)

    def put(name, a, i=0):
        a = np.asarray(a).reshape(-1, P).T
        vec[:, at[name] + i:at[name] + i + a.shape[1]] = a

    def by_part(a):
        return np.asarray(a).reshape(-1, 3, D)[:, hy_order]

    put("norm_g", norm_g)
    put("final_g", final_g)
    put("hy_b_in", by_part(hy_b_in))
    put("hy_conv_w", by_part(hy_conv_w[0]))
    put("hy_conv_b", by_part(hy_conv_b))
    put("hy_skip", hy_skip)
    put("hy_b_out", hy_b_out)
    put("ml_conv_w", ml_conv_w)
    put("ml_conv_b", ml_conv_b)
    put("ml_norm_g", ml_norm_g)
    put("ml_skip", ml_skip)
    put("ada_b", ada_b)
    vec[:, at["cond"]:at["cond"] + 16] = np.stack([np.asarray(c_ctx), np.asarray(c)[0]]).reshape(2, KT, P).transpose(
        2, 1, 0).reshape(P, 16)
    vec[:FILT, at["f_freq"]:at["f_freq"] + 2] = np.asarray(hy_f_freq)[0].T
    vec[:FILT, at["f_b1"]] = hy_f_b1[0]
    vec[:FILT, at["f_b2"]] = hy_f_b2[0]
    vec[:HEADS, at["b_gate"]:at["b_gate"] + 4] = np.asarray(ml_b_gate)[0].reshape(4, HEADS).T
    vec[:, at["mean_w"]] = 1.0 / D
    vec[:, at["eps_norm"]] = 1e-6
    vec[:, at["eps_ml"]] = 1e-5
    vec[:, at["eps_filt"]] = 1e-12
    vec[:, at["neg_t"]:at["neg_t"] + 2] = -const["t_norm"].reshape(2, P).T
    vec[:, at["tap_mask"]:at["tap_mask"] + 2] = 1.0
    vec[0, at["tap_mask"]] = 0.0
    vec[:, at["one"]] = 1.0
    for g in range(4):
        for cd in range(2):
            vec[32 * g + cd, at["cond_sel"] + cd] = 1.0

    fsmall = np.zeros((P, 384), f)
    fsmall[:EMB, 0:FILT] = hy_f_w1[0]
    fsmall[:EMB, FILT:FILT + 256] = const["feats"].T
    fsmall[:FILT, FILT + 256:FILT + 320] = hy_f_w2[0]

    tokens = np.concatenate([np.asarray(ctx)[0], np.asarray(x)[0]]).T.reshape(KT, P, TOK).transpose(1, 0, 2)

    def diagonal(w):
        w = np.asarray(w)[0].reshape(IT, 32, 4, 4)
        out = np.zeros((IT, 32, 4, 32, 4), f)
        for b in range(32):
            out[:, b, :, b, :] = w[:, b]
        return out.reshape(IT, P, P)

    diag3 = np.stack([diagonal(w) for w in (ml_w_q, ml_w_k, ml_w_v)])
    bd = diag3.reshape(3, HEADS, HT, P, P).transpose(1, 3, 2, 0, 4)
    bdt = diag3.transpose(3, 0, 1, 2)
    wg = np.asarray(ml_w_gate)[0].reshape(3, IT, P, 16).transpose(2, 0, 1, 3)
    return {
        "w_stream": w_stream, "ada_stream": ada_stream, "vec": vec, "ident": np.eye(P, dtype=f),
        "ones": np.ones((P, P), f), "fsmall": fsmall, "dft_f": const["dft_f"], "dft_i": const["dft_i"],
        "w3aug": np.concatenate([np.asarray(hy_f_w3)[0], np.asarray(hy_f_b3)]),
        "log_decay": np.asarray(hy_log_decay).reshape(1, -1), "tokens": tokens, "pos": const["pos"],
        "bdt": bdt, "wg": wg, "bd": bd, "mask": const["mask"],
    }


def kernel(**inputs):
    import concourse.bacc as _bacc
    from concourse.bass_utils import run_bass_kernel_spmd as _run

    arrays = {k: np.ascontiguousarray(v) for k, v in lay_out(**{k: np.asarray(v) for k, v in inputs.items()}).items()}
    nc = _bacc.Bacc("TRN2", target_bir_lowering=False, num_devices=1)
    dram = {k: nc.dram_tensor(k + "_dram", a.shape, mybir.dt.from_np(a.dtype), kind="ExternalInput").ap()
            for k, a in arrays.items()}
    dram["out"] = nc.dram_tensor("out_dram", (P, KT, LAT), F32, kind="ExternalOutput").ap()
    build(nc, dram)
    r = _run(nc, [{k + "_dram": a for k, a in arrays.items()}], core_ids=[0])
    out = r.results[0]["out_dram"]
    return out.transpose(1, 0, 2).reshape(D, LAT).T.reshape(1, LAT, D)
```

```python
import math
from contextlib import ExitStack

import numpy as np

import concourse.bass as bass
from concourse import mybir

F32 = mybir.dt.float32
F32R = mybir.dt.float32r
ALU = mybir.AluOpType
ACT = mybir.ActivationFunctionType

P = 128
D = 1024
KT = D // P
CTX = 256
LAT = 256
TOK = CTX + LAT
FF = 2816
FT = FF // P
NFI = FF // 256
NFO = FT // 2
NORM_EPS = 1e-6
BLK = 2048
INNER = 2 * D
HEADS = 4
DH = INNER // HEADS
HT = DH // P
IT = INNER // P
FILT = 64
EMB = 33
BANDS = (EMB - 1) // 2
NSUB = 6
ADA_PAIRS = 6
ALLC, LATC = slice(0, TOK), slice(CTX, TOK)
SEQS = ((slice(0, CTX), 0), (slice(CTX, TOK), 1))

G_FFN = [0, 49, 82, 139]
G_HYIN, G_HYOUT, G_MLUP, G_MLDN = 33, 45, 115, 131
N_BLOCKS = 172


def column_places():
    at, n = {}, 0
    for name, k in (("norm_g", 48), ("final_g", 8), ("hy_b_in", 24), ("hy_conv_w", 72), ("hy_conv_b", 24),
                    ("hy_skip", 16), ("hy_b_out", 8), ("ml_conv_w", 48), ("ml_conv_b", 16), ("ml_norm_g", 16),
                    ("ml_skip", 16), ("ada_b", 144), ("cond", 16), ("f_freq", 2), ("f_b1", 1), ("f_b2", 1),
                    ("b_gate", 4), ("mean_w", 1), ("eps_norm", 1), ("eps_ml", 1), ("eps_filt", 1),
                    ("neg_t", 2), ("tap_mask", 2), ("one", 1), ("cond_sel", 2), ("warm", 1)):
        at[name] = n
        n += k
    return at, n


def build(nc, dram):
    at, n_vec = column_places()
    with ExitStack() as ctx:
        place = [-(-nc.sbuf_base // 64) * 64]

        def fixed(name, shape, dt=F32):
            n = int(np.prod(shape[1:])) * 4
            t = nc.alloc_sbuf_tensor_at(name, shape, dt, offset=place[0])
            place[0] += -(-n // 32) * 32
            return t

        def over(name, shape, offset, dt=F32):
            return nc.alloc_sbuf_tensor_at(name, shape, dt, offset=offset)

        def sem(name):
            return ctx.enter_context(nc.semaphore(name))

        h = fixed("h", [P, KT, TOK])
        act_at = place[0]
        act_hi = fixed("act_hi", [P, KT, TOK], F32R)
        act_lo = fixed("act_lo", [P, KT, TOK], F32R)
        w_raw = fixed("w_raw", [P, 2, BLK])
        w_hi = fixed("w_hi", [P, 2, BLK], F32R)
        w_lo_at = place[0]
        w_lo = fixed("w_lo", [P, 2, BLK], F32R)
        ada_at = place[0]
        ada_raw = fixed("ada_raw", [P, 2, 4, 512])
        scr_at = place[0]
        scratch = fixed("scratch", [P, 24, TOK])
        tmp_at = place[0]
        place[0] += 8192
        kst_at = place[0]
        place[0] += 32768
        vec = fixed("vec", [P, n_vec])
        mods = fixed("mods", [P, 144, 2])
        coef_a = fixed("coef_a", [P, NSUB, KT, 2])
        coef_g = fixed("coef_g", [P, NSUB, KT, 2])
        ident = fixed("ident", [P, P])
        ones = fixed("ones", [P, P])
        cols4 = fixed("cols4", [P, 2, 4])
        cond_pad = fixed("cond_pad", [P, KT, 32])
        w_comb = fixed("w_comb", [P, IT, 2, 16])
        rnorm = fixed("rnorm", [P, 2, KT])
        assert place[0] <= nc.sbuf_usable_end, place[0] - nc.sbuf_usable_end

        def col(name, i=0, n=1):
            return vec[:, at[name] + i:at[name] + i + n]

        hidden = scratch
        silu_g = over("silu_g", [P, 2, TOK], tmp_at)
        ada_part = over("ada_part", [P, 512], tmp_at + 4096)
        nrm = scr_at + 32768
        tn = over("tn", [P, 4, TOK], nrm)
        sq = over("sq", [P, 2, TOK], nrm + 8192)
        diag = over("diag", [P, 4, P], nrm + 12288)
        sq_sum = over("sq_sum", [P, TOK], nrm + 14336)
        w3aug = over("w3aug", [P, 4096], scr_at)
        edecay = over("edecay", [P, 4096], scr_at + 16384)
        pos = over("pos", [P, KT, LAT], scr_at + 32768)
        window = over("window", [P, 2, 2, 512], w_lo_at + 4 * BLK)
        dft_f = over("dft_f", [P, 2, 2, 256], act_at)
        fk = over("fk", [P, 2, 2, 512], act_at + 4096)
        fsd = over("fsd", [P, 2, 2, 512], act_at + 12288)
        fsq = over("fsq", [P, 2, 2, 512], act_at + 20480)
        fmlp = over("fmlp", [P, 4, 256], act_at + 28672)
        fsmall = over("fsmall", [P, 384], tmp_at)
        kst = over("kst", [P, 2, 4, D], kst_at)
        hyp = scratch
        pad = over("pad", [P, 2, 2, 258], tmp_at)
        dft_h = over("dft_h", [P, 2, 2, 256], act_at + 24576)
        dft_i = over("dft_i", [P, 2, 2, 256], act_at + 28672)
        zt = over("zt", [P, 2, 2, 512], act_at)
        zf = over("zf", [P, 2, 4, 512], act_at + 8192)
        pwa = over("pwa", [P, 2, 512], tmp_at)
        gb = over("gb", [P, KT, 2], tmp_at + 6144)
        gate_t = over("gate_t", [P, 4, 256], tmp_at)
        pwb = over("pwb", [P, 2, 512], tmp_at + 4096)
        wg4 = over("wg4", [P, 3, IT, 4, 16], kst_at)
        w4 = over("w4", [P, 3, IT, 4], kst_at + 24576)
        v_tok = over("v_tok", [P, 4, INNER], kst_at)
        score = over("score", [P, HEADS, 2, TOK], scr_at)
        xs = over("xs", [P, IT, LAT], scr_at + 16384)
        k_head = over("k_head", [P, HT, TOK], scr_at + 32768)
        q_head = over("q_head", [P, HT, LAT], scr_at + 40960)
        xc = over("xc", [P, 2, TOK], scr_at + 45056)
        bd = over("bd", [P, 2, HT, 3, P], ada_at)
        zs = over("zs", [P, IT, LAT], scr_at + 32768)
        row_i = over("row_i", [P, 2, TOK], tmp_at)
        row_f = over("row_f", [P, 2, TOK], tmp_at + 4096)
        row_c = over("row_c", [P, 2, TOK], ada_at)
        row_d = over("row_d", [P, 2, TOK], ada_at + 4096)
        row_e = over("row_e", [P, 2, TOK], ada_at + 8192)
        row_g = over("row_g", [P, 2, TOK], ada_at + 12288)
        gsum = over("gsum", [P, TOK], ada_at + 12288)
        mask = over("mask", [P, 2, 2, LAT], act_at)
        pd = [over("pd0", [P, 2, TOK], act_at + 4096), over("pd1", [P, 2, TOK], ada_at + 4096)]
        score_b = over("score_b", [P, HEADS, 2, LAT], tmp_at)
        ht = [over(f"ht{j}", [P, INNER], act_at + 8192 + 16384 * j) for j in range(2)]
        pt = over("pt", [P, 2, 4, P], act_at + 16384)
        pc = over("pc", [P, TOK], act_at + 20480)
        acols = over("acols", [P, 256], act_at + 22528)
        ym = over("ym", [P, IT, LAT], scr_at)
        out_sb = over("out_sb", [P, KT, LAT], scr_at)

        ps = ctx.enter_context(nc.psum_tensor("ps", [P, 8, 512], F32))

        s_const, s_tok, s_pos = sem("const_loaded"), sem("tokens_loaded"), sem("pos_loaded")
        s_mlp, s_w3, s_decay, s_fdft = sem("mlp_loaded"), sem("w3_loaded"), sem("decay_loaded"), sem("filter_dft_loaded")
        s_dft, s_bdt, s_mask, s_out = sem("dft_loaded"), sem("gate_w_loaded"), sem("mask_loaded"), sem("out_stored")
        w_loaded = [sem("w_loaded0"), sem("w_loaded1")]
        w_hi_done, w_lo_done, w_used = sem("w_hi_done"), sem("w_lo_done"), sem("w_used")
        ada_loaded = [sem("ada_loaded0"), sem("ada_loaded1")]
        ada_used, ada_evac, ada_cols, ada_mods = sem("ada_used"), sem("ada_evac"), sem("ada_cols"), sem("ada_mods")
        cond_zero, cond_ready = sem("cond_zero"), sem("cond_ready")
        h_ready, sq_ready, ss_done, std_ready = sem("h_ready"), sem("sq_ready"), sem("ss_done"), sem("std_ready")
        rstd_ready, diag_ready, rb_ready = sem("rstd_ready"), sem("diag_ready"), sem("rb_ready")
        tn_ready, uhi_ready, u_ready = sem("tn_ready"), sem("uhi_ready"), sem("u_ready")
        sq_added, in_free = sem("sq_added"), sem("in_free")
        coef_ready, silu_done, mul_done = sem("coef_ready"), sem("silu_done"), sem("mul_done")
        in_hi, in_lo, y_done = sem("in_hi"), sem("in_lo"), sem("y_done")
        f_pe, f_act, f_dve = sem("filter_pe"), sem("filter_act"), sem("filter_dve")
        pad_zero, pad_ready, conv_step = sem("pad_zero"), sem("pad_ready"), sem("conv_step")
        t_done, t_evac, fwd_done, fwd_evac = sem("t_done"), sem("t_evac"), sem("fwd_done"), sem("fwd_evac")
        pw_done, inv_done, z_done, hy_step = sem("pw_done"), sem("inv_done"), sem("z_done"), sem("hy_step")
        comb_step = sem("comb_step")
        masked = sem("masked")
        bd_loaded = [sem("bd_loaded0"), sem("bd_loaded1")]
        xm_ready, xc_step, xc_ready, xs_done = sem("xm_ready"), sem("xc_step"), sem("xc_ready"), sem("xs_done")
        kq_done, kq_evac, v_done, v_evac, qkv_done = (
            sem("kq_done"), sem("kq_evac"), sem("v_done"), sem("v_evac"), sem("qkv_done"))
        sc_done, sc_evac, z_evac = sem("sc_done"), sem("sc_evac"), sem("z_evac")
        sel_done, row_act, row_dve = sem("sel_done"), sem("row_act"), sem("row_dve")
        rcol_done, rcol_ready, bc_done, a_dve, a_exp = (
            sem("rcol_done"), sem("rcol_ready"), sem("bc_done"), sem("a_dve"), sem("a_exp"))
        pt_done, pt_evac, pv_done, pv_evac, stat_done = (
            sem("pt_done"), sem("pt_evac"), sem("pv_done"), sem("pv_evac"), sem("stat_done"))
        hn_norm = sem("hn_norm")
        hn_std, hn_ready, hnt_done, ym_step, ym_ready = (
            sem("hn_std"), sem("hn_ready"), sem("hnt_done"), sem("ym_step"), sem("ym_ready"))
        out_ready = sem("out_ready")

        IN_BEFORE = [0, 11, 15, 26, 37, 45]
        OUT_BLOCKS = [G_FFN[0] + 22, G_HYOUT, G_FFN[1] + 22, G_FFN[2] + 22, G_MLDN, G_FFN[3] + 22]
        OUT_N = [NFO, 4, NFO, NFO, 8, NFO]
        NORM_BLOCKS = [0] + [g + n for g, n in zip(OUT_BLOCKS, OUT_N)]

        def inv_bank(st):
            return 0 if st == 7 else 4

        ROW = {s: i + 1 for i, s in enumerate(
            ("zero", "gsum0", "gsum1", "i0", "f0", "i1", "f1", "abs", "lf", "cum0", "cum1", "cum2", "cum3", "g",
             "max0", "max1", "max2", "max3", "m"))}
        PE_F = {s: i + 1 for i, s in enumerate(
            ["mlp0", "mlp1"] + [f"{s}{u}" for u in range(4) for s in ("taps", "re", "im", "sums")])}
        ACT_F = {s: i + 1 for i, s in enumerate(
            ["sin0", "sin1", "decay0", "window0"]
            + [f"{s}{u + (s in ('decay', 'window'))}" for u in range(4)
               for s in ("squares", "decay", "window", "re", "im", "sums") if u < 3 or s not in ("decay", "window")]
            + ["std"])}
        DVE_F = {s: i + 1 for i, s in enumerate(
            ["ones_row"] + [f"arg{g}_{k}" for g in range(2) for k in range(7)]
            + [f"{s}{u}" for u in range(4) for s in ("taps", "sum", "diff", "half", "all")] + ["rstd"])}
        A_STEPS = 9
        R = slice(0, HEADS)

        block = ctx.enter_context(nc.Block())

        @block.sync
        def _(sp):
            def load_w(g, i=0):
                if g >= 2:
                    sp.wait_ge(w_lo_done, g - 1 + 2 * i)
                src = dram["w_stream"][g] if isinstance(i, int) else \
                    dram["w_stream"][bass.ds(g + 2 * i, 1)].rearrange("a p n -> (a p) n")
                sp.dma_start(w_raw[:, g % 2, :], src).then_inc(w_loaded[g % 2], 16)

            def load_pairs(g, n):
                with sp.Fori(0, n) as i:
                    load_w(g, i)
                    load_w(g + 1, i)

            sp.dma_start(fsmall[:], dram["fsmall"]).then_inc(s_mlp, 16)
            sp.dma_start(vec[:], dram["vec"]).then_inc(s_mlp, 16)
            sp.dma_start(w3aug[0:FILT + 1, :], dram["w3aug"]).then_inc(s_w3, 16)
            sp.dma_start(edecay[:], dram["log_decay"].to_broadcast([P, 4096])).then_inc(s_decay, 16)
            sp.dma_start(dft_f[:], dram["dft_f"]).then_inc(s_fdft, 16)
            sp.dma_start(ones[:], dram["ones"]).then_inc(s_const, 16)
            sp.dma_start(ident[:], dram["ident"]).then_inc(s_const, 16)
            sp.wait_ge(f_pe, PE_F["taps1"])
            sp.dma_start(h[:], dram["tokens"]).then_inc(s_tok, 16)
            sp.wait_ge(f_pe, PE_F["im1"])
            sp.dma_start(pos[:], dram["pos"]).then_inc(s_pos, 16)
            sp.wait_ge(f_pe, PE_F["sums1"])
            load_w(0)
            sp.wait_ge(f_pe, PE_F["im2"])
            load_w(1)
            load_pairs(2, 22)
            load_w(46)
            sp.wait_ge(w_used, G_HYOUT)
            sp.dma_start(dft_h[:], dram["dft_f"]).then_inc(s_dft, 16)
            sp.dma_start(dft_i[:], dram["dft_i"]).then_inc(s_dft, 16)
            load_w(47)
            load_w(48)
            sp.wait_ge(pw_done, 8)
            for kind in range(3):
                sp.dma_start(wg4[:, kind], dram["wg4"][kind]).then_inc(s_bdt, 16)
            sp.dma_start(w4[:], dram["w4"]).then_inc(s_bdt, 16)
            load_pairs(49, 33)
            sp.wait_ge(ada_used, 2 * ADA_PAIRS * NSUB)
            sp.dma_start(bd[:, 0], dram["bd"][0]).then_inc(bd_loaded[0], 16)
            sp.dma_start(bd[:, 1], dram["bd"][1]).then_inc(bd_loaded[1], 16)
            for g in range(115, 121):
                load_w(g)
            sp.wait_ge(qkv_done, 4)
            sp.dma_start(bd[:, 0], dram["bd"][2]).then_inc(bd_loaded[0], 16)
            for g in range(121, 124):
                load_w(g)
            sp.wait_ge(qkv_done, 8)
            sp.dma_start(bd[:, 1], dram["bd"][3]).then_inc(bd_loaded[1], 16)
            load_pairs(124, 4)
            load_w(132)
            sp.wait_ge(w_used, G_MLDN)
            sp.dma_start(mask[:], dram["mask"]).then_inc(s_mask, 16)
            load_pairs(133, 19)
            load_w(171)
            for k in (0, KT // 2):
                sp.wait_ge(out_ready, k + KT // 2)
                sp.dma_start(dram["out"][:, k:k + KT // 2], out_sb[:, k:k + KT // 2]).then_inc(s_out, 16)
            sp.wait_ge(s_out, 32)

        @block.gpsimd
        def _(pool):
            for s in range(2):
                pool.dma_start(ada_raw[:, s], dram["ada_stream"][s]).then_inc(ada_loaded[s], 16)
            with pool.Fori(1, ADA_PAIRS * NSUB) as q:
                for s in range(2):
                    pool.wait_ge(ada_used, 2 * q - 1 + s)
                    pool.dma_start(ada_raw[:, s],
                                   dram["ada_stream"][bass.ds(2 * q + s, 1)].rearrange("a p k n -> (a p) k n")
                                   ).then_inc(ada_loaded[s], 16)

            pool.wait_ge(s_mask, 16)
            pool.wait_ge(row_dve, ROW["g"])
            for it in range(8):
                hd, jt = it // 2, it % 2
                pool.wait_ge(sc_evac, hd + 1)
                pool.tensor_tensor(score_b[:, hd, jt], score[:, hd, jt, LATC], mask[:, 1, jt], ALU.mult).then_inc(masked, 1)
                pool.wait_ge(masked, 2 * it + 1)
                pool.tensor_tensor(score[:, hd, jt, LATC], score[:, hd, jt, LATC], mask[:, 0, jt],
                                   ALU.mult).then_inc(masked, 1)

        @block.scalar
        def _(act):
            def split_w(g, i=0):
                if g >= N_BLOCKS:
                    return
                act.wait_ge(w_loaded[g % 2], 16 * (g // 2 + 1) + 16 * i)
                if g >= 2:
                    act.wait_ge(w_used, g - 1 + 2 * i)
                act.activation(w_hi[:, g % 2, :], w_raw[:, g % 2, :], ACT.Copy).then_inc(w_hi_done, 1)

            def squares(n, cols, tiles=range(KT)):
                if n > 0:
                    act.activation(col("warm"), col("one"), ACT.Sqrt)
                for m in tiles:
                    act.wait_ge(h_ready, 8 * n + m + 1)
                    if m >= 2:
                        act.wait_ge(sq_added, 7 * n + max(m - 2, 1))
                    act.activation(sq[:, m % 2, cols], h[:, m, cols], ACT.Square).then_inc(sq_ready, 1)
                if n > 0:
                    root(n, cols)

            def root(n, cols):
                w = (cols.stop - cols.start) // P
                act.wait_ge(ss_done, n + 1)
                act.activation(cols4[:, 0, 0:w], ps[:, 0, 0:w], ACT.Sqrt, bias=col("eps_norm")).then_inc(std_ready, 1)

            def affine(n, cols):
                act.wait_ge(ada_mods, ADA_PAIRS * n + 2)
                for k in range(KT):
                    act.wait_ge(tn_ready, 8 * n + k + 1)
                    for c, cd in SEQS:
                        if c.start >= cols.start:
                            last = act.activation(act_hi[:, k, c], tn[:, k % 4, c], ACT.Identity,
                                                  bias=mods[:, 24 * n + k, cd:cd + 1])
                    last.then_inc(uhi_ready, 1)

            def ffn_in(f, cols, first_out):
                g0 = G_FFN[f]

                def step(p, i=0):
                    if p > 0 or f > 0:
                        act.wait_ge(mul_done, NFI * f + p + i)
                    act.wait_ge(w_used, g0 + 2 * p + 1 + 2 * i)
                    act.activation(silu_g[:, :, cols], ps[:, 0:2, cols], ACT.Silu).then_inc(silu_done, 1)
                    split_w(g0 + 2 * p + 2, i)
                    if p == NFI - 1:
                        first_out()
                    split_w(g0 + 2 * p + 3, i)

                step(0)
                with act.Fori(0, NFI - 2) as i:
                    step(1, i)
                step(NFI - 1)

            def out_proj(o, cols, src, first_ready):
                g0, nb = OUT_BLOCKS[o], OUT_N[o]

                def split_in(b, i=0):
                    if b < 2:
                        first_ready(act, b)
                    else:
                        act.wait_ge(w_used, g0 + b - 1 + 2 * i)
                        if o == 1:
                            act.wait_ge(z_done, 8)
                        if o == 4:
                            act.wait_ge(ym_ready, b // 2 + 1)
                    s = 2 * (b % 2)
                    act.activation(act_hi[:, s:s + 2, cols], src(b, i), ACT.Copy).then_inc(in_hi, 1)

                def step(b, i=0):
                    split_w(g0 + b + 2, i)
                    if b + 2 < nb:
                        split_in(b + 2, i)

                def first():
                    split_in(0)
                    split_in(1)

                def rest():
                    loops = 0 if o == 4 else (nb - 3) // 2
                    if loops:
                        with act.Fori(0, loops) as i:
                            step(0, i)
                            step(1, i)
                    for b in range(2 * loops, nb - 1):
                        step(b)

                return first, rest

            act.wait_ge(s_mlp, 32)
            act.wait_ge(cond_zero, 1)
            act.activation(cond_pad[:, :, 0:2], col("cond", 0, 16).rearrange("p (k c) -> p k c", c=2),
                           ACT.Silu).then_inc(cond_ready, 1)
            for stage in range(2):
                act.wait_ge(f_dve, DVE_F[f"arg{stage}_6"])
                act.activation(fmlp[0:FILT, 2 + stage, :], fmlp[0:FILT, 0, :], ACT.Sin).then_inc(f_act, 1)

            def windows(u):
                e0 = u // 2 * 2048 + u % 2 * 512
                e = edecay[:, e0:e0 + 2048 - u % 2 * 512].rearrange("p (d c) -> p d c", c=1024)[:, :, 0:512] \
                    if u % 2 == 0 else edecay[:, e0 - 512:e0 + 1536].rearrange("p (d c) -> p d c", c=1024)[:, :, 512:]
                act.activation(e, e, ACT.Exp).then_inc(f_act, 1)
                act.wait_ge(f_act, ACT_F[f"decay{u}"])
                if u > 0:
                    act.wait_ge(f_dve, DVE_F[f"taps{u - 1}"])
                for dr in range(2):
                    for t in range(2):
                        last = act.activation(window[:, dr, t], e[:, dr], ACT.Exp, scale=col("neg_t", t))
                last.then_inc(f_act, 1)

            act.wait_ge(s_decay, 16)
            windows(0)
            for u in range(4):
                o, c = u // 2, u % 2
                act.wait_ge(f_dve, DVE_F[f"taps{u}"])
                if u > 0:
                    act.wait_ge(f_pe, PE_F[f"sums{u - 1}"])
                act.activation(fsq[:], fk[:], ACT.Square).then_inc(f_act, 1)
                if u < 3:
                    windows(u + 1)
                act.wait_ge(f_pe, PE_F[f"re{u}"])
                act.activation(kst[:, o, 0:2, c * 512:c * 512 + 512], ps[:, 6:8, :], ACT.Copy).then_inc(f_act, 1)
                act.wait_ge(f_pe, PE_F[f"im{u}"])
                act.activation(kst[:, o, 2:4, c * 512:c * 512 + 512], ps[:, 6:8, :], ACT.Copy).then_inc(f_act, 1)
                act.wait_ge(f_pe, PE_F[f"sums{u}"])
                act.activation(rnorm[:, o, c * 4:c * 4 + 4], ps[:, 0, 0:4], ACT.Copy).then_inc(f_act, 1)
                if u == 2:
                    squares(0, ALLC, range(0, 4))
                    split_w(0)
                if u == 3:
                    squares(0, ALLC, range(4, KT))
            act.wait_ge(f_act, ACT_F["sums3"])
            act.activation(rnorm[:], rnorm[:], ACT.Sqrt, bias=col("eps_filt")).then_inc(f_act, 1)

            def hidden_tiles(cols):
                return lambda b, i: hidden[:, bass.ds(2 * b + 4 * i, 2), cols]

            def ffn(f, n, cols):
                first, rest = out_proj(n, cols, hidden_tiles(cols), lambda e, b: e.wait_ge(in_free, 2 * f + b + 1))
                ffn_in(f, cols, first)
                rest()
                squares(n + 1, cols)

            root(0, ALLC)
            affine(0, ALLC)
            split_w(1)
            ffn(0, 0, ALLC)
            affine(1, ALLC)
            split_w(G_HYIN + 1)

            def hy_in(j, i=0):
                for t in range(2):
                    tile = 2 * j + t
                    if tile == 0:
                        act.wait_ge(pad_zero, 1)
                    if t == 0:
                        act.wait_ge(w_used, G_HYIN + j + 1 + 2 * i)
                    if j > 0:
                        act.wait_ge(conv_step, 3 * (tile - 1) + 12 * i)
                    act.activation(pad[:, t, :, 1:257],
                                   ps[:, 2 * (j % 2) + t, :].rearrange("p (s n) -> p s n", s=2), ACT.Identity,
                                   bias=vec[:, bass.ds(at["hy_b_in"] + tile + 4 * i, 1)]).then_inc(pad_ready, 1)
                split_w(G_HYIN + j + 2, i)

            hy_in(0)
            hy_in(1)
            with act.Fori(0, 5) as i:
                hy_in(2, i)
                hy_in(3, i)
            for st in range(8):
                act.wait_ge(t_done, st + 1)
                if st >= 2:
                    act.wait_ge(fwd_done, st - 1)
                act.activation(zt[:, st % 2], ps[:, 6:8, :], ACT.Copy).then_inc(t_evac, 1)
                act.wait_ge(fwd_done, st + 1)
                if st >= 2:
                    act.wait_ge(inv_done, st - 1)
                act.activation(zf[:, (st + 1) % 2], ps[:, 0:4, :], ACT.Copy).then_inc(fwd_evac, 1)
            first, rest = out_proj(1, ALLC, lambda b, i: hyp[:, 2 * b:2 * b + 2, :],
                                   lambda e, b: e.wait_ge(z_done, 7))
            first()
            rest()
            squares(2, ALLC)
            affine(2, ALLC)
            split_w(G_FFN[1] + 1)
            ffn(1, 2, ALLC)
            affine(3, ALLC)
            split_w(G_FFN[2] + 1)
            ffn(2, 3, ALLC)
            affine(4, ALLC)
            split_w(G_MLUP + 1)
            for j in range(8):
                for t in range(2):
                    tile = 2 * j + t
                    if tile == 0:
                        act.wait_ge(pad_zero, 2)
                    if t == 0:
                        act.wait_ge(w_used, G_MLUP + j + 1)
                    if j > 0:
                        act.wait_ge(qkv_done, tile - 1)
                    act.activation(pad[:, t, :, 1:257],
                                   ps[:, 2 * (j % 2) + t, :].rearrange("p (s n) -> p s n", s=2),
                                   ACT.Copy).then_inc(xm_ready, 1)
                split_w(G_MLUP + j + 2)
                for t in range(2):
                    act.wait_ge(xc_step, 3 * (2 * j + t) + 3)
                    act.activation(xc[:, t, :], xc[:, t, :], ACT.Silu).then_inc(xc_ready, 1)
                for t in range(2):
                    tile = 2 * j + t
                    act.wait_ge(kq_done, tile + 1)
                    act.activation(q_head[:, tile % HT, :], ps[:, 5, 0:LAT], ACT.Copy)
                    act.activation(k_head[:, tile % HT, :], ps[:, 4, :], ACT.Copy).then_inc(kq_evac, 1)
                    act.wait_ge(v_done, tile + 1)
                    act.activation(v_tok[:, :, tile * P:tile * P + P],
                                   ps[:, 6, :].rearrange("p (a c) -> p a c", a=4), ACT.Copy).then_inc(v_evac, 1)
                if j == 7:
                    split_w(G_MLUP + 10)
                if j % 2:
                    act.wait_ge(sc_done, j // 2 + 1)
                    act.activation(score[:, j // 2], ps[:, 4:6, :], ACT.Copy, scale=DH ** -0.5).then_inc(sc_evac, 1)
            act.wait_ge(xs_done, IT)

            def z_step(j, i=0, split=True):
                act.wait_ge(w_used, G_MLUP + 9 + j + 2 * i)
                act.activation(zs[:, bass.ds(2 * j + 4 * i, 2), :], ps[:, 2 * (j % 2):2 * (j % 2) + 2, LATC],
                               ACT.Silu).then_inc(z_evac, 1)
                if split:
                    split_w(G_MLUP + 10 + j, i)

            z_step(0, split=False)
            z_step(1)
            act.wait_ge(row_dve, ROW["abs"])
            act.activation(row_c[R], row_c[R], ACT.Exp, scale=-1.0).then_inc(row_act, 1)
            act.wait_ge(row_act, 1)
            act.activation(row_c[R], row_c[R], ACT.Ln, bias=col("one")[R]).then_inc(row_act, 1)
            z_step(2)
            z_step(3)
            act.wait_ge(row_dve, ROW["m"])
            act.activation(row_c[R], row_d[R], ACT.Exp, scale=-1.0).then_inc(row_act, 1)
            z_step(4)
            z_step(5)
            z_step(6)
            z_step(7, split=False)
            act.activation(col("warm"), col("one"), ACT.Exp)
            act.wait_ge(rcol_done, 1)
            act.activation(acols[:, 0:16], ps[:, 6, 0:16], ACT.Copy, scale=-1.0)
            act.activation(acols[:, 16:32], ps[:, 6, 16:32], ACT.Copy).then_inc(rcol_ready, 1)
            act.wait_ge(rcol_ready, 1)

            def weights(it):
                hd, jt = it // 2, it % 2
                act.wait_ge(bc_done, hd + 1)
                if it >= 2:
                    act.wait_ge(a_dve, A_STEPS * (it - 1))
                for dr in range(2):
                    c = (dr * 2 + jt) * HEADS + hd
                    act.activation(pd[it % 2][:, dr, :], ps[:, 4 - 2 * (hd % 2) + dr, :], ACT.Exp,
                                   bias=acols[:, c:c + 1]).then_inc(a_exp, 1)

            def values(it):
                act.wait_ge(pv_done, it + 1)
                act.activation(ht[it % 2][:, it // 2 * DH:(it // 2 + 1) * DH], ps[:, 7 - 7 * (it % 2), :],
                               ACT.Copy).then_inc(pv_evac, 1)

            def deviation(g):
                act.wait_ge(stat_done, 8 * (g + 1))
                act.activation(acols[:, 152 + 4 * g:156 + 4 * g],
                               acols[:, 64 + 8 * g:72 + 8 * g].rearrange("p (a b) -> p a b", b=2)[:, :, 1],
                               ACT.Sqrt, bias=col("eps_ml")).then_inc(hn_std, 1)

            def normalize(g):
                act.wait_ge(hn_ready, 2 * g + 2)
                for it in range(4 * g, 4 * g + 4):
                    act.wait_ge(pv_evac, it + 1)
                    hv = ht[it % 2][:, it // 2 * DH:(it // 2 + 1) * DH]
                    act.activation(hv, hv, ACT.Identity, scale=acols[:, 160 + it:161 + it],
                                   bias=acols[:, 176 + it:177 + it]).then_inc(hn_norm, 1)

            weights(0)
            for it in range(8):
                if it >= 2:
                    values(it - 2)
                if it < 7:
                    weights(it + 1)
                act.wait_ge(pt_done, it + 1)
                if it >= 2:
                    act.wait_ge(pv_done, it - 1)
                act.activation(pt[:, it % 2], ps[:, 6 - 5 * (it % 2), :].rearrange("p (a c) -> p a c", a=4),
                               ACT.Copy).then_inc(pt_evac, 1)
                if it == 0:
                    split_w(G_MLUP + 17)
                if it == 6:
                    deviation(0)
            normalize(0)
            values(6)
            values(7)
            deviation(1)
            first, rest = out_proj(4, LATC, lambda b, i: ym[:, bass.ds(2 * b + 4 * i, 2), :],
                                   lambda e, b: e.wait_ge(ym_ready, 1))
            first()
            normalize(1)
            rest()
            squares(5, LATC)
            affine(5, LATC)
            split_w(G_FFN[3] + 1)
            ffn(3, 5, LATC)
        @block.vector
        def _(dve):
            def split_w(g, i=0):
                if g >= N_BLOCKS:
                    return
                dve.wait_ge(w_hi_done, g + 1 + 2 * i)
                dve.tensor_tensor(w_lo[:, g % 2, :], w_raw[:, g % 2, :], w_hi[:, g % 2, :].bitcast(F32),
                                  ALU.subtract).then_inc(w_lo_done, 1)

            def ada_copy(q):
                dve.wait_ge(ada_used, 2 * q + 2)
                if not isinstance(q, int) or q > 0:
                    dve.wait_ge(ada_cols, q)
                dve.tensor_copy(ada_part[:], ps[:, 4, :]).then_inc(ada_evac, 1)

            def ada_bias(q):
                dve.wait_ge(ada_cols, q + 1)
                b = vec[:, bass.ds(at["ada_b"] + 4 * q, 4)].rearrange("p (a b) -> p a b", b=1)
                dve.tensor_tensor(mods[:, bass.ds(4 * q, 4), :], ps[:, 5, 0:8].rearrange("p (a b) -> p a b", b=2),
                                  b.to_broadcast([P, 4, 2]), ALU.add).then_inc(ada_mods, 1)

            def coefs(n):
                dve.wait_ge(ada_mods, ADA_PAIRS * (n + 1))
                g = col("norm_g", 8 * n, 8).rearrange("p (a b) -> p a b", b=1).to_broadcast([P, KT, 2])
                dve.scalar_tensor_tensor(coef_a[:, n], mods[:, 24 * n + 8:24 * n + 16, :], 1.0, g,
                                         ALU.add, ALU.mult).then_inc(coef_ready, 1)
                dve.tensor_scalar(coef_g[:, n], mods[:, 24 * n + 16:24 * n + 24, :], 1.0 if n % 3 == 1 else 0.5,
                                  None, ALU.mult).then_inc(coef_ready, 1)

            def norm(n, cols, final=False, pair=None):
                w = (cols.stop - cols.start) // P
                if n > 0:
                    split_w(NORM_BLOCKS[n])
                dve.wait_ge(std_ready, n + 1)
                dve.reciprocal(cols4[:, 1, 0:w], cols4[:, 0, 0:w]).then_inc(rstd_ready, 1)
                dve.wait_ge(rstd_ready, n + 1)
                dve.tensor_tensor(diag[:, 0:w, :], ident[:].rearrange("p (a c) -> p a c", a=1).to_broadcast([P, w, P]),
                                  cols4[:, 1, 0:w].rearrange("p (t a) -> p t a", a=1).to_broadcast([P, w, P]),
                                  ALU.mult).then_inc(diag_ready, 1)
                if pair is not None:
                    ada_copy(pair)
                dve.wait_ge(rb_ready, n + 1)
                if not final:
                    dve.wait_ge(coef_ready, 2 * n + 2)

                def lo(k):
                    dve.wait_ge(uhi_ready, 8 * n + k + 1)
                    for c, cd in SEQS:
                        if c.start >= cols.start:
                            last = dve.scalar_tensor_tensor(act_lo[:, k, c], tn[:, k % 4, c],
                                                            mods[:, 24 * n + k, cd:cd + 1],
                                                            act_hi[:, k, c].bitcast(F32), ALU.add, ALU.subtract)
                    last.then_inc(u_ready, 1)

                for k in range(KT):
                    if final:
                        dve.scalar_tensor_tensor(out_sb[:, k, :], h[:, k, cols], col("final_g", k), ps[:, 6, cols],
                                                 ALU.mult, ALU.mult).then_inc(out_ready, 1)
                        continue
                    if k >= 4:
                        dve.wait_ge(u_ready, k - 3 + 8 * n)
                    for c, cd in SEQS:
                        if c.start >= cols.start:
                            last = dve.scalar_tensor_tensor(tn[:, k % 4, c], h[:, k, c], coef_a[:, n, k, cd:cd + 1],
                                                            ps[:, 6, c], ALU.mult, ALU.mult)
                    last.then_inc(tn_ready, 1)
                    if k > 0:
                        lo(k - 1)
                if not final:
                    lo(KT - 1)
                if pair is not None:
                    ada_bias(pair)

            def add_squares(n, m, cols):
                dve.wait_ge(sq_ready, 8 * n + m + 1)
                if m > 1:
                    dve.wait_ge(sq_added, 7 * n + m - 1)
                dve.tensor_tensor(sq_sum[:, cols], sq[:, 0, cols] if m == 1 else sq_sum[:, cols],
                                  sq[:, m % 2, cols], ALU.add).then_inc(sq_added, 1)

            def ffn_in(f, cols, first_out, q0=0, n_ada=0):
                g0 = G_FFN[f]

                def step(p, i=0, ada=False):
                    split_w(g0 + 2 * p + 2, i)
                    if p == NFI - 1:
                        first_out()
                    if ada:
                        ada_copy(q0 + p + i)
                    dve.wait_ge(silu_done, NFI * f + p + 1 + i)
                    dve.wait_ge(w_used, g0 + 2 * p + 2 + 2 * i)
                    dve.tensor_tensor(hidden[:, bass.ds(2 * p + 2 * i, 2), cols], silu_g[:, :, cols],
                                      ps[:, 2:4, cols], ALU.mult).then_inc(mul_done, 1)
                    split_w(g0 + 2 * p + 3, i)
                    if ada:
                        ada_bias(q0 + p + i)

                step(0, 0, n_ada > 0)
                if n_ada > 1:
                    with dve.Fori(0, n_ada - 1) as i:
                        step(1, i, True)
                first = max(n_ada, 1)
                if first < NFI - 1:
                    with dve.Fori(0, NFI - 1 - first) as i:
                        step(first, i)
                step(NFI - 1)

            def out_proj(o, cols):
                g0, nb = OUT_BLOCKS[o], OUT_N[o]

                def split_in(b, src, i=0):
                    dve.wait_ge(in_hi, IN_BEFORE[o] + b + 1 + 2 * i)
                    s = 2 * (b % 2)
                    dve.tensor_tensor(act_lo[:, s:s + 2, cols], src(b, i), act_hi[:, s:s + 2, cols].bitcast(F32),
                                      ALU.subtract).then_inc(in_lo, 1)

                if o == 1:
                    src = lambda b, i: hyp[:, 2 * b:2 * b + 2, :]
                elif o == 4:
                    src = lambda b, i: ym[:, bass.ds(2 * b + 4 * i, 2), :]
                else:
                    src = lambda b, i: hidden[:, bass.ds(2 * b + 4 * i, 2), cols]

                def step(b, i=0):
                    split_w(g0 + b + 2, i)
                    if b + 2 < nb:
                        split_in(b + 2, src, i)

                def first():
                    split_in(0, src)
                    split_in(1, src)

                def rest():
                    if o < 5:
                        coefs(o + 1)
                    loops = 0 if o == 4 else (nb - 3) // 2
                    if loops:
                        with dve.Fori(0, loops) as i:
                            step(0, i)
                            step(1, i)
                    for b in range(2 * loops, nb - 2):
                        step(b)
                    dve.wait_ge(coef_ready, 2 * o + 2)
                    for m in range(KT):
                        dve.wait_ge(y_done, 8 * o + m + 1)
                        for c, cd in SEQS:
                            if c.start >= cols.start:
                                last = dve.scalar_tensor_tensor(h[:, m, c], ps[:, m, c], coef_g[:, o, m, cd:cd + 1],
                                                                h[:, m, c], ALU.mult, ALU.add)
                        last.then_inc(h_ready, 1)
                        if m >= 2:
                            add_squares(o + 1, m - 1, cols)
                    add_squares(o + 1, KT - 1, cols)

                return first, rest

            def ffn(f, n, cols, q0=0, n_ada=0):
                first, rest = out_proj(n, cols)
                ffn_in(f, cols, first, q0, n_ada)
                rest()

            dve.memset(cond_pad[:], 0.0).then_inc(cond_zero, 1)
            dve.memset(fmlp[FILT:FILT + 1, 3, :], 1.0).then_inc(f_dve, 1)
            dve.wait_ge(s_mlp, 32)
            two_pi = 2 * math.pi
            c1 = 6.28125
            c2 = float(np.float32(np.round((two_pi - c1) * 2 ** 22) / 2 ** 22))
            c3 = float(np.float32(two_pi - c1 - c2))
            pi32 = float(np.nextafter(np.float32(math.pi), np.float32(0)))
            magic = 1.5 * 2 ** 23
            X, N = fmlp[0:FILT, 0, :], fmlp[0:FILT, 1, :]
            for stage in range(2):
                n = DVE_F[f"arg{stage}_0"] - 1
                dve.wait_ge(f_pe, PE_F[f"mlp{stage}"])
                bias = col("f_b1" if stage == 0 else "f_b2")[0:FILT]
                dve.tensor_scalar(X, ps[0:FILT, 2, 0:256], bias, col("f_freq", stage)[0:FILT],
                                  ALU.add, ALU.mult).then_inc(f_dve, 1)
                dve.wait_ge(f_dve, n + 1)
                dve.tensor_scalar(N, X, 1.0 / two_pi, magic, ALU.mult, ALU.add).then_inc(f_dve, 1)
                dve.wait_ge(f_dve, n + 2)
                dve.tensor_scalar(N, N, magic, None, ALU.subtract).then_inc(f_dve, 1)
                dve.wait_ge(f_dve, n + 3)
                dve.scalar_tensor_tensor(X, N, -c1, X, ALU.mult, ALU.add).then_inc(f_dve, 1)
                dve.wait_ge(f_dve, n + 4)
                dve.scalar_tensor_tensor(X, N, -c2, X, ALU.mult, ALU.add).then_inc(f_dve, 1)
                dve.wait_ge(f_dve, n + 5)
                dve.scalar_tensor_tensor(X, N, -c3, X, ALU.mult, ALU.add).then_inc(f_dve, 1)
                dve.wait_ge(f_dve, n + 6)
                dve.tensor_scalar(X, X, pi32, -pi32, ALU.min, ALU.max).then_inc(f_dve, 1)
            for u in range(4):
                dve.wait_ge(f_pe, PE_F[f"taps{u}"])
                dve.wait_ge(f_act, ACT_F[f"window{u}"])
                if u > 0:
                    dve.wait_ge(f_act, ACT_F[f"squares{u - 1}"])
                for t in range(2):
                    dve.tensor_tensor(fk[:, 0, t], ps[:, 2 * t, :], window[:, 0, t], ALU.mult)
                    last = dve.scalar_tensor_tensor(fk[:, 1, t], ps[:, 2 * t + 1, :], col("tap_mask", t),
                                                    window[:, 1, t], ALU.mult, ALU.mult)
                last.then_inc(f_dve, 1)
                dve.wait_ge(f_dve, DVE_F[f"taps{u}"])
                if u > 0:
                    dve.wait_ge(f_pe, PE_F[f"im{u - 1}"])
                dve.tensor_tensor(fsd[:, 0], fk[:, 0], fk[:, 1], ALU.add).then_inc(f_dve, 1)
                dve.tensor_tensor(fsd[:, 1], fk[:, 0], fk[:, 1], ALU.subtract).then_inc(f_dve, 1)
                if u > 0:
                    ada_bias(2 * u)
                else:
                    ada_copy(0)
                    ada_bias(0)
                ada_copy(2 * u + 1)
                dve.wait_ge(f_act, ACT_F[f"squares{u}"])
                dve.tensor_tensor(fsq[:, 0], fsq[:, 0], fsq[:, 1], ALU.add).then_inc(f_dve, 1)
                dve.wait_ge(f_dve, DVE_F[f"half{u}"])
                dve.tensor_tensor(fsq[:, 0, 0], fsq[:, 0, 0], fsq[:, 0, 1], ALU.add).then_inc(f_dve, 1)
                ada_bias(2 * u + 1)
                if u == 2:
                    dve.wait_ge(s_tok, 16)
                    dve.wait_ge(s_pos, 16)
                    for m in range(KT):
                        dve.tensor_tensor(h[:, m, LATC], h[:, m, LATC], pos[:, m, :], ALU.add).then_inc(h_ready, 1)
                if u == 2:
                    for m in range(1, 4):
                        add_squares(0, m, ALLC)
                    split_w(0)
                ada_copy(2 * u + 2)
            for m in range(4, KT):
                add_squares(0, m, ALLC)
            ada_bias(8)
            dve.wait_ge(f_act, ACT_F["std"])
            dve.reciprocal(rnorm[:], rnorm[:]).then_inc(f_dve, 1)
            coefs(0)
            norm(0, ALLC, pair=9)
            split_w(1)
            ffn(0, 0, ALLC, q0=10, n_ada=8)

            norm(1, ALLC, pair=18)
            split_w(G_HYIN + 1)
            dve.memset(pad[:], 0.0).then_inc(pad_zero, 1)

            def conv(dst, t, w0, wn, b0, tile, i, per, step_sem):
                def c(first):
                    return vec[:, bass.ds(first + tile + per * i, 1)]

                n = 3 * tile + 3 * per * i
                dve.tensor_scalar(dst, pad[:, t, :, 1:257], c(w0 + wn), c(b0), ALU.mult, ALU.add).then_inc(step_sem, 1)
                dve.wait_ge(step_sem, n + 1)
                dve.scalar_tensor_tensor(dst, pad[:, t, :, 0:256], c(w0), dst, ALU.mult, ALU.add).then_inc(step_sem, 1)
                dve.wait_ge(step_sem, n + 2)
                dve.scalar_tensor_tensor(dst, pad[:, t, :, 2:258], c(w0 + 2 * wn), dst,
                                         ALU.mult, ALU.add).then_inc(step_sem, 1)

            def hy_in(j, i=0):
                for t in range(2):
                    tile = 2 * j + t
                    dve.wait_ge(pad_ready, tile + 1 + 4 * i)
                    dst = hyp[:, bass.ds(tile + 4 * i, 1), :].rearrange("p a (s n) -> p (a s) n", s=2)
                    conv(dst, t, at["hy_conv_w"], 24, at["hy_conv_b"], tile, i, 4, conv_step)
                split_w(G_HYIN + j + 2, i)

            steps = [0]

            def own(ins):
                steps[0] += 1
                ins.then_inc(hy_step, 1)

            hy_in(0)
            dve.wait_ge(coef_ready, 4)
            b_out = col("hy_b_out", 0, 8).rearrange("p (a b) -> p a b", b=1).to_broadcast([P, KT, 2])
            own(dve.tensor_tensor(gb[:], coef_g[:, 1], b_out, ALU.mult))
            dve.wait_ge(hy_step, steps[0])
            for m in range(KT):
                for c, cd in SEQS:
                    ins = dve.tensor_scalar(h[:, m, c], h[:, m, c], gb[:, m, cd:cd + 1], None, ALU.add)
            own(ins)
            hy_in(1)
            with dve.Fori(0, 5) as i:
                hy_in(2, i)
                hy_in(3, i)
            dve.wait_ge(conv_step, 72)
            ada_copy(19)
            ada_bias(19)

            def pointwise(st):
                o, c = st // 4, st % 2
                z, k = zf[:, (st + 1) % 2], kst[:, o, :, c * 512:c * 512 + 512]
                zr, zi, kr, ki = z[:, 0:2], z[:, 2:4], k[:, 0:2], k[:, 2:4]
                if st > 0:
                    dve.wait_ge(pw_done, st)
                if st > 1:
                    dve.wait_ge(z_done, st - 1)
                dve.wait_ge(fwd_evac, st + 1)
                dve.tensor_tensor(pwa[:], zi, ki, ALU.mult)
                own(dve.tensor_tensor(pwb[:], zr, ki, ALU.mult))
                dve.wait_ge(hy_step, steps[0])
                own(dve.tensor_tensor(zr, zr, kr, ALU.mult))
                own(dve.tensor_tensor(zi, zi, kr, ALU.mult))
                dve.wait_ge(hy_step, steps[0] - 1)
                dve.tensor_tensor(zr, zr, pwa[:], ALU.subtract)
                dve.wait_ge(hy_step, steps[0])
                dve.tensor_tensor(zi, zi, pwb[:], ALU.add).then_inc(pw_done, 1)

            def gate(st):
                o, s, c = st // 4, st // 2 % 2, st % 2
                v = hyp[:, 4 * c:4 * c + 4, s * 256:s * 256 + 256]
                x = hyp[:, 8 + 8 * o + 4 * c:12 + 8 * o + 4 * c, s * 256:s * 256 + 256]
                dve.wait_ge(pw_done, min(st + 2, 8))
                if st > 0:
                    dve.wait_ge(z_done, st)
                for ct in range(4):
                    ins = dve.tensor_scalar(gate_t[:, ct], v[:, ct], col("hy_skip", 8 * o + 4 * c + ct), None, ALU.mult)
                own(ins)
                dve.wait_ge(inv_done, st + 1)
                dve.wait_ge(hy_step, steps[0])
                for ct in range(4):
                    ins = dve.scalar_tensor_tensor(gate_t[:, ct], ps[:, inv_bank(st) + ct // 2, ct % 2 * 256:ct % 2 * 256 + 256],
                                                   rnorm[:, o, 4 * c + ct:4 * c + ct + 1], gate_t[:, ct],
                                                   ALU.mult, ALU.add)
                own(ins)
                dve.wait_ge(hy_step, steps[0])
                dve.tensor_tensor(v, gate_t[:], x, ALU.mult).then_inc(z_done, 1)

            for st in range(9):
                if st < 8:
                    pointwise(st)
                if 0 < st < 8:
                    gate(st - 1)
            first, rest = out_proj(1, ALLC)
            first()
            gate(7)
            rest()
            norm(2, ALLC, pair=20)
            split_w(G_FFN[1] + 1)
            ffn(1, 2, ALLC, q0=21, n_ada=9)
            norm(3, ALLC, pair=30)
            split_w(G_FFN[2] + 1)
            dve.wait_ge(s_bdt, 64)
            for kind in range(3):
                w = w4[:, kind].rearrange("p t (j a) -> p t j a", a=1).to_broadcast([P, IT, 4, 16])
                ins = dve.tensor_tensor(wg4[:, kind], wg4[:, kind], w, ALU.mult)
            ins.then_inc(comb_step, 1)
            dve.wait_ge(comb_step, 1)
            for kind in range(3):
                ins = dve.tensor_tensor(wg4[:, kind, :, 0:2], wg4[:, kind, :, 0:2], wg4[:, kind, :, 2:4], ALU.add)
            ins.then_inc(comb_step, 1)
            dve.wait_ge(comb_step, 2)
            for kind in range(3):
                ins = dve.tensor_tensor(wg4[:, kind, :, 0], wg4[:, kind, :, 0], wg4[:, kind, :, 1], ALU.add)
            ins.then_inc(comb_step, 1)
            dve.wait_ge(comb_step, 3)
            dve.tensor_tensor(w_comb[:, :, 0], wg4[:, 0, :, 0], wg4[:, 1, :, 0], ALU.add)
            dve.tensor_copy(w_comb[:, :, 1], wg4[:, 2, :, 0]).then_inc(comb_step, 1)
            ffn(2, 3, ALLC, q0=31, n_ada=5)
            norm(4, ALLC)
            split_w(G_MLUP + 1)
            dve.memset(pad[:], 0.0).then_inc(pad_zero, 1)
            for j in range(8):
                for t in range(2):
                    tile = 2 * j + t
                    dve.wait_ge(xm_ready, tile + 1)
                    if j > 0:
                        dve.wait_ge(qkv_done, tile - 1)
                        dve.wait_ge(xs_done, tile - 1)
                    dst = xc[:, t, :].rearrange("p (s n) -> p s n", s=2)
                    conv(dst, t, at["ml_conv_w"], 16, at["ml_conv_b"], tile, 0, 0, xc_step)
                split_w(G_MLUP + j + 2)
                for t in range(2):
                    tile = 2 * j + t
                    dve.wait_ge(xc_ready, tile + 1)
                    dve.tensor_scalar(xs[:, tile, :], xc[:, t, LATC], col("ml_skip", tile), None,
                                      ALU.mult).then_inc(xs_done, 1)
            split_w(G_MLUP + 10)
            dve.wait_ge(qkv_done, IT)
            dve.memset(cond_pad[:], 0.0).then_inc(row_dve, 1)
            zeros = cond_pad[R].rearrange("p k c -> p (k c)")
            for g in range(2):
                dve.tensor_copy(gsum[32 * g:32 * g + 16, :], ps[32 * g:32 * g + 16, 7, :]).then_inc(row_dve, 1)
            split_w(G_MLUP + 11)
            dve.wait_ge(sel_done, 2)
            for dr in range(2):
                dve.tensor_scalar(row_i[R, dr], ps[R, 4 + 2 * dr, :], col("b_gate", 2 * dr)[R], None,
                                  ALU.add).then_inc(row_dve, 1)
                dve.tensor_scalar(row_f[R, dr], ps[R, 5 + 2 * dr, :], col("b_gate", 2 * dr + 1)[R], None,
                                  ALU.add).then_inc(row_dve, 1)
            dve.wait_ge(row_dve, ROW["f1"])
            dve.scalar_tensor_tensor(row_c[R], row_f[R], -1.0, row_f[R], ALU.mult, ALU.max).then_inc(row_dve, 1)
            dve.wait_ge(row_act, 2)
            dve.scalar_tensor_tensor(row_f[R], row_f[R], 0.0, row_c[R], ALU.min, ALU.subtract).then_inc(row_dve, 1)

            def scans(out, src, second, op, steps_of):
                dve.wait_ge(row_dve, ROW[steps_of[0]] - 1)
                for dr in range(2):
                    for part, c in enumerate((slice(0, CTX), slice(CTX, TOK))):
                        def view(x):
                            return x[:, ::-1] if dr else x
                        if part == 0:
                            init = 0.0
                        else:
                            init = out[R, dr, CTX - 1:CTX] if dr == 0 else out[R, dr, 0:1]
                            dve.wait_ge(row_dve, ROW[steps_of[2 * dr]])
                        s = view(src[R, dr, c])
                        dve.tensor_tensor_scan(view(out[R, dr, c]), s, zeros if second is None else s, init,
                                               op, op).then_inc(row_dve, 1)

            scans(row_d, row_f, None, ALU.add, ("cum0", "cum1", "cum2", "cum3"))
            dve.wait_ge(row_dve, ROW["cum3"])
            dve.tensor_tensor(row_g[R], row_i[R], row_d[R], ALU.subtract).then_inc(row_dve, 1)
            split_w(G_MLUP + 12)
            scans(row_e, row_g, True, ALU.max, ("max0", "max1", "max2", "max3"))
            dve.wait_ge(row_dve, ROW["max3"])
            dve.tensor_tensor(row_d[R], row_d[R], row_e[R], ALU.add).then_inc(row_dve, 1)
            for g in range(G_MLUP + 13, G_MLUP + 17):
                split_w(g)
            dve.wait_ge(rcol_ready, 1)
            dve.wait_ge(sc_evac, HEADS)
            rc = acols[:, 0:32].rearrange("p (q d j e) -> p q d j e", q=2, d=2, j=2)

            def stats(it):
                dve.wait_ge(pv_evac, it + 1)
                hv = ht[it % 2][:, it // 2 * DH:(it // 2 + 1) * DH]
                dve.bn_stats(acols[:, 104 + 6 * it:110 + 6 * it], hv).then_inc(stat_done, 1)
                dve.wait_ge(stat_done, 2 * it + 1)
                dve.bn_aggr(acols[:, 64 + 2 * it:66 + 2 * it], acols[:, 104 + 6 * it:110 + 6 * it]).then_inc(stat_done, 1)

            def inverse_std(g):
                a, b = 4 * g, 4 * g + 4
                dve.wait_ge(hn_std, g + 1)
                dve.reciprocal(acols[:, 160 + a:160 + b], acols[:, 152 + a:152 + b]).then_inc(hn_ready, 1)
                dve.wait_ge(hn_ready, 2 * g + 1)
                dve.scalar_tensor_tensor(acols[:, 176 + a:176 + b],
                                         acols[:, 64 + 2 * a:64 + 2 * b].rearrange("p (a b) -> p a b", b=2)[:, :, 0],
                                         -1.0, acols[:, 160 + a:160 + b], ALU.mult, ALU.mult).then_inc(hn_ready, 1)

            def gate_heads(g, halves):
                dve.wait_ge(z_evac, 8)
                for half in halves:
                    c0 = 8 * g + 4 * half
                    for ct in range(c0, c0 + 4):
                        dve.wait_ge(hnt_done, (ct | 1) + 1)
                        dve.scalar_tensor_tensor(ym[:, ct, :], ps[:, 2 + ct // 2 % 4, ct % 2 * 256:ct % 2 * 256 + 256],
                                                 col("ml_norm_g", ct), xs[:, ct, :], ALU.mult, ALU.add).then_inc(ym_step, 1)
                    dve.wait_ge(ym_step, c0 + 4)
                    dve.tensor_tensor(ym[:, c0:c0 + 4], ym[:, c0:c0 + 4], zs[:, c0:c0 + 4], ALU.mult).then_inc(ym_ready, 1)

            for it in range(8):
                hd, jt = it // 2, it % 2
                n = A_STEPS * it
                qn = acols[:, 32 + 2 * it:34 + 2 * it]
                qn_b = acols[:, 168 + it:169 + it]
                rd = acols[:, 48 + 2 * it:50 + 2 * it]
                p = pd[it % 2]
                dve.wait_ge(masked, 2 * it + 2)
                dve.wait_ge(a_exp, 2 * it + 1)
                dve.scalar_tensor_tensor(p[:, 0, :], p[:, 0, :], 1.0, score[:, hd, jt, :], ALU.min, ALU.mult,
                                         accum_out=qn[:, 0:1]).then_inc(a_dve, 1)
                dve.wait_ge(a_exp, 2 * it + 2)
                dve.scalar_tensor_tensor(p[:, 1, 0:CTX], p[:, 1, 0:CTX], 1.0, score[:, hd, jt, 0:CTX], ALU.min, ALU.mult,
                                         accum_out=qn[:, 1:2]).then_inc(a_dve, 1)
                dve.scalar_tensor_tensor(p[:, 1, LATC], p[:, 1, LATC], 1.0, score_b[:, hd, jt], ALU.min, ALU.mult,
                                         accum_out=qn_b).then_inc(a_dve, 1)
                dve.wait_ge(a_dve, n + 3)
                dve.tensor_tensor(qn[:, 1:2], qn[:, 1:2], qn_b, ALU.add).then_inc(a_dve, 1)
                dve.wait_ge(a_dve, n + 4)
                dve.scalar_tensor_tensor(rd, qn, -1.0, qn, ALU.mult, ALU.max).then_inc(a_dve, 1)
                dve.wait_ge(a_dve, n + 5)
                dve.tensor_tensor(rd, rd, rc[:, 1, :, jt, hd], ALU.max).then_inc(a_dve, 1)
                dve.wait_ge(a_dve, n + 6)
                dve.reciprocal(rd, rd).then_inc(a_dve, 1)
                dve.wait_ge(a_dve, n + 7)
                if it > 0:
                    dve.wait_ge(pt_done, it)
                dve.tensor_scalar(pc[:], p[:, 0, :], rd[:, 0:1], None, ALU.mult).then_inc(a_dve, 1)
                dve.wait_ge(a_dve, n + 8)
                dve.scalar_tensor_tensor(pc[:], p[:, 1, :], rd[:, 1:2], pc[:], ALU.mult, ALU.add).then_inc(a_dve, 1)
                if it == 1:
                    split_w(G_MLUP + 17)
                if it == 7:
                    inverse_std(0)
                if it >= 2:
                    stats(it - 2)

            stats(6)
            gate_heads(0, (0,))
            stats(7)
            inverse_std(1)
            first, rest = out_proj(4, LATC)
            first()
            gate_heads(0, (1,))
            gate_heads(1, (0, 1))
            rest()
            norm(5, LATC)
            split_w(G_FFN[3] + 1)
            ffn(3, 5, LATC)
            norm(6, LATC, final=True)

        @block.tensor
        def _(pe):
            def keep_warm(bank, n):
                for _ in range(n):
                    pe.matmul(ps[0:32, bank, 0:256], cond_pad[:, 0, :], cond_pad[:].rearrange("p k c -> p (k c)"),
                              start=True, stop=True)

            def product(out, w, x, start, stop):
                (wh, wl), (xh, xl) = w, x
                pe.matmul(out, wh, xh, start=start, stop=False)
                pe.matmul(out, wh, xl, start=False, stop=False)
                return pe.matmul(out, wl, xh, start=False, stop=stop)

            def in_block(g, i, bank, cols, norm_n=None, frees=False):
                pe.wait_ge(w_lo_done, g + 1 + 2 * i)
                s = g % 2
                wh = w_hi[:, s, :].rearrange("p (k c) -> p k c", c=256)
                wl = w_lo[:, s, :].rearrange("p (k c) -> p k c", c=256)
                for k in range(KT):
                    if norm_n is not None and k < 2:
                        c = [slice(t * P, t * P + P) for t in range(2)]
                        pe.wait_ge(uhi_ready, 8 * norm_n + k + 1)
                        for t in range(2):
                            out = ps[:, bank + t, cols]
                            pe.matmul(out, wh[:, k, c[t]], act_hi[:, k, cols], start=k == 0, stop=False)
                            pe.matmul(out, wl[:, k, c[t]], act_hi[:, k, cols], start=False, stop=False)
                        pe.wait_ge(u_ready, 8 * norm_n + k + 1)
                        for t in range(2):
                            mm = pe.matmul(ps[:, bank + t, cols], wh[:, k, c[t]], act_lo[:, k, cols],
                                           start=False, stop=False)
                        continue
                    if norm_n is not None:
                        pe.wait_ge(u_ready, 8 * norm_n + k + 1)
                    for t in range(2):
                        c = slice(t * P, t * P + P)
                        mm = product(ps[:, bank + t, cols], (wh[:, k, c], wl[:, k, c]),
                                     (act_hi[:, k, cols], act_lo[:, k, cols]), k == 0, k == KT - 1)
                    if frees and k in (1, 3):
                        mm.then_inc(in_free, 1)
                mm.then_inc(w_used, 1)

            def ada_half(q, s, block_done=False):
                if s == 0 and (not isinstance(q, int) or q > 0):
                    pe.wait_ge(ada_evac, q)
                pe.wait_ge(ada_loaded[s], 16 * q + 16)
                for k in range(4):
                    mm = pe.matmul(ps[32 * k:32 * k + 32, 4, :], cond_pad[:, 4 * s + k, :], ada_raw[:, s, k, :],
                                   start=s == 0, stop=s == 1)
                    if k == 0 and block_done:
                        mm.then_inc(w_used, 1)
                mm.then_inc(ada_used, 1)

            def ada_pair(q):
                ada_half(q, 0)
                ada_half(q, 1)

            def ada_turn(q):
                pe.wait_ge(ada_evac, q + 1)
                if not isinstance(q, int) or q > 0:
                    pe.wait_ge(ada_mods, q)
                for t in range(4):
                    mm = pe.matmul(ps[:, 5, 2 * t:2 * t + 2], ada_part[:, t * P:t * P + P], col("cond_sel", 0, 2),
                                   start=True, stop=True)
                mm.then_inc(ada_cols, 1)

            def square_sums(n, cols, block_done=False):
                pe.wait_ge(sq_added, 7 * n + KT - 1)
                for t in range((cols.stop - cols.start) // P):
                    c = slice(cols.start + t * P, cols.start + t * P + P)
                    mm = pe.matmul(ps[:, 0, t:t + 1], sq_sum[:, c], col("mean_w"), start=True, stop=True)
                    if block_done:
                        mm.then_inc(w_used, 1)
                        block_done = False
                mm.then_inc(ss_done, 1)

            def rms_rows(n, cols):
                pe.wait_ge(diag_ready, n + 1)
                w = (cols.stop - cols.start) // P
                pe.matmul(ps[:, 6, cols], ones[:], diag[:, 0:w, :], start=True, stop=True).then_inc(rb_ready, 1)

            def chain(n, cols, pair):
                if pair is not None:
                    pe.wait_ge(h_ready, 8 * n + 5)
                    ada_half(pair, 0, block_done=True)
                    ada_half(pair, 1)
                pe.wait_ge(h_ready, 8 * n + 8)
                keep_warm(7, 2 if pair is not None else 3)
                square_sums(n, cols, block_done=pair is None)
                keep_warm(7, 5)
                rms_rows(n, cols)
                if pair is not None:
                    ada_turn(pair)
                keep_warm(7, 2 if pair is not None else 3)

            def ffn_in(f, n, cols, q0=0, n_ada=0):
                g0 = G_FFN[f]

                def step(p, i=0, ada=False):
                    if p > 0:
                        pe.wait_ge(silu_done, NFI * f + p + i)
                    in_block(g0 + 2 * p, i, 0, cols, n if p == 0 else None)
                    if ada:
                        ada_pair(q0 + p + i)
                    if p > 0:
                        pe.wait_ge(mul_done, NFI * f + p + i)
                    in_block(g0 + 2 * p + 1, i, 2, cols, frees=p == NFI - 1)
                    if ada:
                        ada_turn(q0 + p + i)

                step(0, 0, n_ada > 0)
                if n_ada > 1:
                    with pe.Fori(0, n_ada - 1) as i:
                        step(1, i, True)
                first = max(n_ada, 1)
                if first < NFI - 1:
                    with pe.Fori(0, NFI - 1 - first) as i:
                        step(first, i)
                step(NFI - 1)

            def out_proj(o, cols, pairs, pair=None, between=None):
                g0, nb = OUT_BLOCKS[o], OUT_N[o]
                f = {0: 0, 2: 1, 3: 2, 5: 3}.get(o)
                if pairs:
                    pe.wait_ge(ada_mods, pairs)

                def operands(b):
                    s, sw = b % 2, (g0 + b) % 2
                    wh = w_hi[:, sw, :].rearrange("p (k c) -> p k c", c=D)
                    wl = w_lo[:, sw, :].rearrange("p (k c) -> p k c", c=D)
                    return lambda k, m: ((wh[:, k, m * P:m * P + P], wl[:, k, m * P:m * P + P]),
                                         (act_hi[:, 2 * s + k, cols], act_lo[:, 2 * s + k, cols]))

                def step(b, i=0):
                    pe.wait_ge(w_lo_done, g0 + b + 1 + 2 * i)
                    pe.wait_ge(in_lo, IN_BEFORE[o] + b + 1 + 2 * i)
                    ops = operands(b)
                    order = range(KT)
                    if b == 0:
                        order = {1: (2, 3, 4, 5, 6, 7, 0, 1), 4: (6, 7, 0, 1, 2, 3, 4, 5)}.get(
                            o, (4, 5, 6, 7, 0, 1, 2, 3))
                    turns = [(k, m) for k in range(2) for m in order] if o != 4 or b else \
                        [(k, m) for m in order for k in range(2)]
                    for k, m in turns:
                        if b == 0 and k == 0:
                            if o == 1 and m == 0:
                                pe.wait_ge(z_done, 8)
                            elif o == 4 and m == 6:
                                pe.wait_ge(pv_evac, 8)
                            elif o == 4 and 2 <= m <= 5:
                                if m == 2:
                                    between()
                                pe.wait_ge(ym_step, 2 * m + 6)
                            elif f is not None and m == 0:
                                pe.wait_ge(mul_done, NFI * (f + 1))
                        w, x = ops(k, m)
                        mm = product(ps[:, m, cols], w, x, b == 0 and k == 0, False)
                    mm.then_inc(w_used, 1)

                step(0)
                loops = 0 if o == 4 else (nb - 3) // 2
                if loops:
                    with pe.Fori(0, loops) as i:
                        step(1, i)
                        step(2, i)
                for b in range(1 + 2 * loops, nb - 1):
                    step(b)
                b = nb - 1
                pe.wait_ge(w_lo_done, g0 + b + 1)
                pe.wait_ge(in_lo, IN_BEFORE[o] + b + 1)
                ops = operands(b)
                for m in range(KT):
                    for k in range(2):
                        w, x = ops(k, m)
                        mm = product(ps[:, m, cols], w, x, False, k == 1)
                    mm.then_inc(y_done, 1)
                chain(o + 1, cols, pair)

            pe.wait_ge(cond_ready, 1)
            keep_warm(7, 1)
            pe.wait_ge(s_mlp, 32)
            pe.matmul(ps[0:FILT, 2, 0:256], fsmall[0:EMB, 0:FILT], fsmall[0:EMB, FILT:FILT + 256],
                      start=True, stop=True).then_inc(f_pe, 1)
            keep_warm(7, 3)
            ada_half(0, 0)
            pe.wait_ge(f_act, ACT_F["sin0"])
            pe.matmul(ps[0:FILT, 2, 0:256], fsmall[0:FILT, FILT + 256:FILT + 320], fmlp[0:FILT, 2, :],
                      start=True, stop=True).then_inc(f_pe, 1)
            def taps(u):
                if u == 0:
                    pe.wait_ge(f_act, ACT_F["sin1"])
                    pe.wait_ge(s_w3, 16)
                else:
                    pe.wait_ge(f_act, ACT_F[f"sums{u - 1}"])
                for t in range(2):
                    for dr in range(2):
                        w0 = u // 2 * 2048 + dr * 1024 + u % 2 * 512
                        mm = pe.matmul(ps[:, 2 * t + dr, :], fmlp[0:FILT + 1, 3, t * P:t * P + P],
                                       w3aug[0:FILT + 1, w0:w0 + 512], start=True, stop=True)
                mm.then_inc(f_pe, 1)

            def spectrum(u, part):
                pe.wait_ge(f_dve, DVE_F[("sum", "diff")[part] + str(u)])
                if part == 1:
                    pe.wait_ge(f_act, ACT_F[f"re{u}"])
                elif u > 0:
                    pe.wait_ge(f_act, ACT_F[f"im{u - 1}"])
                else:
                    pe.wait_ge(s_fdft, 16)
                for m in range(2):
                    for t in range(2):
                        mm = pe.matmul(ps[:, 6 + m, :], dft_f[:, part, t, m * P:m * P + P],
                                       fsd[:, part, t], start=t == 0, stop=t == 1)
                mm.then_inc(f_pe, 1)

            keep_warm(7, 6)
            taps(0)
            keep_warm(7, 2)
            ada_half(0, 1)
            keep_warm(7, 3)
            for u in range(4):
                if u > 0:
                    ada_pair(2 * u + 1)
                spectrum(u, 0)
                ada_turn(2 * u + 1 if u > 0 else 0)
                spectrum(u, 1)
                if u == 0:
                    ada_pair(1)
                    keep_warm(1, 2)
                    ada_turn(1)
                    keep_warm(1, 2)
                    pe.wait_ge(s_const, 32)
                pe.wait_ge(f_dve, DVE_F[f"all{u}"])
                for ct in range(4):
                    mm = pe.matmul(ps[:, 0, ct:ct + 1], fsq[:, 0, 0, ct * P:ct * P + P], col("one"),
                                   start=True, stop=True)
                mm.then_inc(f_pe, 1)
                if u < 2:
                    keep_warm(1, 2 + 4 * u)
                ada_pair(2 * u + 2)
                if u < 3:
                    taps(u + 1)
                    ada_turn(2 * u + 2)
            pe.wait_ge(f_act, ACT_F["sums3"])
            ada_turn(8)
            square_sums(0, ALLC)
            ada_pair(9)
            rms_rows(0, ALLC)
            ada_turn(9)
            keep_warm(7, 2)
            ffn_in(0, 0, ALLC, q0=10, n_ada=8)
            out_proj(0, ALLC, 18, 18)
            def hy_in(j, i=0):
                if j >= 2:
                    pe.wait_ge(pad_ready, 2 * j - 2 + 4 * i)
                in_block(G_HYIN + j, i, 2 * (j % 2), ALLC, 1 if j == 0 else None)

            hy_in(0)
            hy_in(1)
            with pe.Fori(0, 5) as i:
                hy_in(2, i)
                hy_in(3, i)

            def turn(st):
                o, s, c = st // 4, st // 2 % 2, st % 2
                if o == 0:
                    pe.wait_ge(conv_step, 24)
                else:
                    pe.wait_ge(z_done, st - 3)
                if st > 0:
                    pe.wait_ge(t_evac, st)
                else:
                    pe.wait_ge(rb_ready, 2)
                for t in range(2):
                    for ct in range(4):
                        n0 = s * 256 + t * P
                        mm = pe.transpose(ps[:, 6 + t, ct * P:ct * P + P], hyp[:, 4 * c + ct, n0:n0 + P], ident[:])
                mm.then_inc(t_done, 1)

            def forward(st):
                pe.wait_ge(t_evac, st + 1)
                if st > 0:
                    pe.wait_ge(fwd_evac, st)
                else:
                    pe.wait_ge(s_dft, 32)
                for part in range(2):
                    for m in range(2):
                        for t in range(2):
                            mm = pe.matmul(ps[:, 2 * part + m, :], dft_h[:, part, t, m * P:m * P + P],
                                           zt[:, st % 2, t, :], start=t == 0, stop=t == 1)
                mm.then_inc(fwd_done, 1)

            def inverse(st):
                pe.wait_ge(pw_done, st + 1)
                if 0 < st < 7:
                    pe.wait_ge(z_done, st)
                for ct in range(4):
                    for q in range(4):
                        mm = pe.matmul(ps[:, inv_bank(st) + ct // 2, ct % 2 * 256:ct % 2 * 256 + 256],
                                       zf[:, (st + 1) % 2, q, ct * P:ct * P + P], dft_i[:, q // 2, q % 2, :],
                                       start=q == 0, stop=q == 3)
                mm.then_inc(inv_done, 1)

            turn(0)
            ada_pair(19)
            for st in range(9):
                if st < 7:
                    turn(st + 1)
                if st == 0:
                    ada_turn(19)
                if st < 8:
                    forward(st)
                if st > 0:
                    inverse(st - 1)
            out_proj(1, ALLC, 20, 20)
            ffn_in(1, 2, ALLC, q0=21, n_ada=9)
            out_proj(2, ALLC, 30, 30)
            ffn_in(2, 3, ALLC, q0=31, n_ada=5)
            out_proj(3, ALLC, 36)

            def up(j):
                if 2 <= j <= 9:
                    pe.wait_ge(xm_ready, 2 * j - 2)
                in_block(G_MLUP + j, 0, 2 * (j % 2), ALLC if j < 8 else LATC, 4 if j == 0 else None)

            pe.wait_ge(comb_step, 4)

            def qkv(j):
                for t in range(2):
                    tile = 2 * j + t
                    hd, ht_i = tile // HT, tile % HT
                    b = bd[:, hd % 2, ht_i]
                    if ht_i == 0:
                        pe.wait_ge(bd_loaded[hd % 2], 16 * (hd // 2 + 1))
                        if hd > 0:
                            pe.wait_ge(sc_evac, hd)
                    pe.wait_ge(xc_ready, tile + 1)
                    if tile > 0:
                        pe.wait_ge(kq_evac, tile)
                    pe.matmul(ps[:, 5, 0:LAT], b[:, 0], xc[:, t, LATC], start=True, stop=True)
                    pe.matmul(ps[:, 4, :], b[:, 1], xc[:, t, :], start=True, stop=True).then_inc(kq_done, 1)
                    if tile > 0:
                        pe.wait_ge(v_evac, tile)
                    for s in range(4):
                        n0 = 1 + (s % 2) * P
                        mm = pe.matmul(ps[:, 6, s * P:s * P + P], pad[:, t, s // 2, n0:n0 + P], b[:, 2],
                                       start=True, stop=True)
                    mm.then_inc(v_done, 1)
                    pe.matmul(ps[0:16, 7, :], w_comb[:, tile, 0, :], xc[:, t, :], start=tile == 0, stop=tile == IT - 1,
                              skip_group_check=True)
                    pe.matmul(ps[32:48, 7, :], w_comb[:, tile, 1, :], pad[:, t, :, 1:257], start=tile == 0,
                              stop=tile == IT - 1, skip_group_check=True).then_inc(qkv_done, 1)

            up(0)
            for j in range(8):
                up(j + 1)
                qkv(j)
                if j % 2:
                    hd = j // 2
                    pe.wait_ge(kq_evac, HT * (hd + 1))
                    for jt in range(2):
                        for k in range(HT):
                            mm = pe.matmul(ps[:, 4 + jt, :], q_head[:, k, jt * P:jt * P + P], k_head[:, k, :],
                                           start=k == 0, stop=k == HT - 1)
                    mm.then_inc(sc_done, 1)
            up(9)
            pe.wait_ge(row_dve, ROW["gsum1"])
            pe.wait_ge(sc_evac, HEADS)
            pe.wait_ge(v_evac, IT)
            for g in range(2):
                if g == 1:
                    pe.wait_ge(sel_done, 1)
                for r in range(4):
                    a = slice(32 * g, 32 * g + 16)
                    mm = pe.matmul(ps[R, 4 + r, :], ident[a, 32 * g + 4 * r:32 * g + 4 * r + 4], gsum[a, :],
                                   start=g == 0, stop=g == 1)
                mm.then_inc(sel_done, 1)

            def z_block(j, i):
                pe.wait_ge(z_evac, j - 1 + 2 * i)
                in_block(G_MLUP + 8 + j, i, 2 * (j % 2), LATC)

            with pe.Fori(0, 3) as i:
                z_block(2, i)
                z_block(3, i)
            def spread(hd):
                if hd >= 2:
                    pe.wait_ge(a_exp, 4 * (hd - 1))
                for dr in range(2):
                    mm = pe.matmul(ps[:, 4 - 2 * (hd % 2) + dr, :], ident[R, hd:hd + 1].to_broadcast([HEADS, P]),
                                   row_g[R, dr, :], start=True, stop=True)
                mm.then_inc(bc_done, 1)

            pe.wait_ge(row_act, 3)
            spread(0)
            for q, rows in enumerate((row_e, row_c)):
                for dr in range(2):
                    for jt in range(2):
                        o0 = ((q * 2 + dr) * 2 + jt) * HEADS
                        mm = pe.transpose(ps[:, 6, o0:o0 + HEADS], rows[R, dr, CTX + jt * P:CTX + jt * P + P],
                                          ident[R, 0:HEADS])
            mm.then_inc(rcol_done, 1)
            pe.wait_ge(z_evac, 8)

            def turn_p(it):
                pe.wait_ge(a_dve, A_STEPS * (it + 1))
                if it >= 2:
                    pe.wait_ge(pt_evac, it - 1)
                elif it == 0:
                    pe.wait_ge(rcol_ready, 1)
                for q in range(4):
                    mm = pe.transpose(ps[:, 6 - 5 * (it % 2), q * P:q * P + P], pc[:, q * P:q * P + P], ident[:])
                mm.then_inc(pt_done, 1)

            def turn_h(g):
                pe.wait_ge(a_exp, 16)
                for ct in range(8 * g, 8 * g + 8):
                    pe.wait_ge(hn_norm, 2 * (ct // HT + 1))
                    if g == 1:
                        pe.wait_ge(ym_step, 2 * (ct // 2) - 6)
                    for jt in range(2):
                        mm = pe.transpose(ps[:, 2 + ct // 2 % 4, ct % 2 * 256 + jt * P:ct % 2 * 256 + jt * P + P],
                                          ht[jt][:, ct * P:ct * P + P], ident[:])
                    mm.then_inc(hnt_done, 1)

            spread(1)
            turn_p(0)
            for it in range(8):
                hd = it // 2
                if it < 7:
                    turn_p(it + 1)
                if it % 2 and hd < 2:
                    spread(hd + 2)
                if it == 7:
                    turn_h(0)
                pe.wait_ge(pt_evac, it + 1)
                if it >= 2:
                    pe.wait_ge(pv_evac, it - 1)
                for q in range(4):
                    mm = pe.matmul(ps[:, 7 - 7 * (it % 2), :], pt[:, it % 2, q, :], v_tok[:, q, hd * DH:(hd + 1) * DH],
                                   start=q == 0, stop=q == 3)
                mm.then_inc(pv_done, 1)
            out_proj(4, LATC, 0, between=lambda: turn_h(1))
            ffn_in(3, 5, LATC)
            out_proj(5, LATC, 0)


def constants():
    f = np.float32
    n = CTX
    t = np.arange(n, dtype=f)
    t_norm = (t / f(n - 1)).astype(f)
    bands = np.linspace(1e-4, BANDS - 1, BANDS, dtype=f)
    ang = ((f(2.0 * math.pi / n) * t)[:, None] * bands[None, :]).astype(f)
    feats = np.concatenate([t_norm[:, None], np.cos(ang), -np.sin(ang)], axis=-1).astype(f)
    theta = np.pi * (2 * np.arange(n)[None, :] + 1) * np.arange(n)[:, None] / (2 * n)
    fwd = np.stack([np.cos(theta), -np.sin(theta)]).reshape(2, 2, P, n).transpose(2, 0, 1, 3)
    inv = (np.stack([np.cos(theta.T), -np.sin(theta.T)]) / n).reshape(2, 2, P, n).transpose(2, 0, 1, 3)
    quarter = D // 4
    omega = (1.0 / (f(10000.0) ** (np.arange(quarter, dtype=f) / f(quarter)))).astype(f)
    rows = LAT // 64
    ang_r, ang_c = np.arange(rows, dtype=f)[:, None] * omega, np.arange(64, dtype=f)[:, None] * omega
    row_emb = np.concatenate([np.sin(ang_r), np.cos(ang_r)], axis=-1)
    col_emb = np.concatenate([np.sin(ang_c), np.cos(ang_c)], axis=-1)
    emb = np.concatenate([np.broadcast_to(row_emb[:, None, :], (rows, 64, D // 2)),
                          np.broadcast_to(col_emb[None, :, :], (rows, 64, D // 2))], axis=-1).reshape(LAT, D)
    j, s = np.arange(LAT)[:, None], np.arange(LAT)[None, :]
    mask = np.stack([s <= j, s >= j]).astype(f).reshape(2, 2, P, LAT).transpose(2, 0, 1, 3)
    return {"t_norm": t_norm, "feats": feats, "dft_f": fwd.astype(f), "dft_i": inv.astype(f),
            "pos": emb.astype(f).T.reshape(KT, P, LAT).transpose(1, 0, 2), "mask": mask}


def lay_out(x, c, ctx, c_ctx, ada_w, ada_b, norm_g, final_g, ffn_w_in, ffn_w_out, hy_w_in, hy_b_in, hy_conv_w,
            hy_conv_b, hy_f_w1, hy_f_b1, hy_f_w2, hy_f_b2, hy_f_w3, hy_f_b3, hy_f_freq, hy_log_decay, hy_skip,
            hy_w_out, hy_b_out, ml_w_up, ml_conv_w, ml_conv_b, ml_w_q, ml_w_k, ml_w_v, ml_w_gate, ml_b_gate,
            ml_norm_g, ml_skip, ml_w_down):
    f = np.float32
    const = constants()
    at, n_vec = column_places()

    def in_blocks(w):
        return w.reshape(KT, P, -1, 256).transpose(2, 1, 0, 3).reshape(-1, P, BLK)

    def out_blocks(w):
        return w.reshape(-1, 2, P, D).transpose(0, 2, 1, 3).reshape(-1, P, BLK)

    def ffn_blocks(layer, half):
        w = in_blocks(ffn_w_in[layer, half])
        pairs = np.stack([w[:NFI], w[NFI:]], axis=1).reshape(2 * NFI, P, BLK)
        return [pairs, out_blocks(ffn_w_out[layer, half])]

    hy_order = [2, 0, 1]
    hy_in = in_blocks(hy_w_in[0]).reshape(3, 4, P, BLK)[hy_order].reshape(12, P, BLK)
    w_stream = np.concatenate(ffn_blocks(0, 0) + [hy_in, out_blocks(hy_w_out[0])] + ffn_blocks(0, 1)
                              + ffn_blocks(1, 0) + [in_blocks(ml_w_up[0]), out_blocks(ml_w_down[0])]
                              + ffn_blocks(1, 1))
    assert w_stream.shape[0] == N_BLOCKS
    ada_stream = np.asarray(ada_w).reshape(2, 2, 4, P, -1, 512).transpose(0, 4, 1, 3, 2, 5).reshape(-1, P, 4, 512)

    vec = np.zeros((P, n_vec), f)

    def put(name, a, i=0):
        a = np.asarray(a).reshape(-1, P).T
        vec[:, at[name] + i:at[name] + i + a.shape[1]] = a

    def by_part(a):
        return np.asarray(a).reshape(-1, 3, D)[:, hy_order]

    put("norm_g", norm_g)
    put("final_g", final_g)
    put("hy_b_in", by_part(hy_b_in))
    put("hy_conv_w", by_part(hy_conv_w[0]))
    put("hy_conv_b", by_part(hy_conv_b))
    put("hy_skip", hy_skip)
    put("hy_b_out", hy_b_out)
    put("ml_conv_w", ml_conv_w)
    put("ml_conv_b", ml_conv_b)
    put("ml_norm_g", ml_norm_g)
    put("ml_skip", ml_skip)
    put("ada_b", ada_b)
    vec[:, at["cond"]:at["cond"] + 16] = np.stack([np.asarray(c_ctx), np.asarray(c)[0]]).reshape(2, KT, P).transpose(
        2, 1, 0).reshape(P, 16)
    vec[:FILT, at["f_freq"]:at["f_freq"] + 2] = np.asarray(hy_f_freq)[0].T
    vec[:FILT, at["f_b1"]] = hy_f_b1[0]
    vec[:FILT, at["f_b2"]] = hy_f_b2[0]
    vec[:HEADS, at["b_gate"]:at["b_gate"] + 4] = np.asarray(ml_b_gate)[0].reshape(4, HEADS).T
    vec[:, at["mean_w"]] = 1.0 / D
    vec[:, at["eps_norm"]] = NORM_EPS
    vec[:, at["eps_ml"]] = 1e-5
    vec[:, at["eps_filt"]] = 1e-12
    vec[:, at["neg_t"]:at["neg_t"] + 2] = -const["t_norm"].reshape(2, P).T
    vec[:, at["tap_mask"]:at["tap_mask"] + 2] = 1.0
    vec[0, at["tap_mask"]] = 0.0
    vec[:, at["one"]] = 1.0
    for g in range(4):
        for cd in range(2):
            vec[32 * g + cd, at["cond_sel"] + cd] = 1.0

    fsmall = np.zeros((P, 384), f)
    fsmall[:EMB, 0:FILT] = hy_f_w1[0]
    fsmall[:EMB, FILT:FILT + 256] = const["feats"].T
    fsmall[:FILT, FILT + 256:FILT + 320] = hy_f_w2[0]

    tokens = np.concatenate([np.asarray(ctx)[0], np.asarray(x)[0]]).T.reshape(KT, P, TOK).transpose(1, 0, 2)

    def diagonal(w):
        w = np.asarray(w)[0].reshape(IT, 32, 4, 4)
        out = np.zeros((IT, 32, 4, 32, 4), f)
        for b in range(32):
            out[:, b, :, b, :] = w[:, b]
        return out.reshape(IT, P, P)

    diag3 = np.stack([diagonal(w) for w in (ml_w_q, ml_w_k, ml_w_v)])
    bd = diag3.reshape(3, HEADS, HT, P, P).transpose(1, 3, 2, 0, 4)
    w4 = np.stack([np.asarray(w)[0].reshape(IT, P, 4) for w in (ml_w_q, ml_w_k, ml_w_v)]).transpose(2, 0, 1, 3)
    wg4 = np.repeat(np.asarray(ml_w_gate)[0].reshape(3, IT, 32, 1, 4, 16), 4, axis=3).reshape(3, IT, P, 4, 16)
    wg4 = wg4.transpose(0, 2, 1, 3, 4)
    return {
        "w_stream": w_stream, "ada_stream": ada_stream, "vec": vec, "ident": np.eye(P, dtype=f),
        "ones": np.ones((P, P), f), "fsmall": fsmall, "dft_f": const["dft_f"], "dft_i": const["dft_i"],
        "w3aug": np.concatenate([np.asarray(hy_f_w3)[0], np.asarray(hy_f_b3)]),
        "log_decay": np.asarray(hy_log_decay).reshape(1, -1), "tokens": tokens, "pos": const["pos"],
        "wg4": wg4, "w4": w4, "bd": bd, "mask": const["mask"],
    }


def kernel(**inputs):
    import concourse.bacc as _bacc
    from concourse.bass_utils import run_bass_kernel_spmd as _run

    arrays = {k: np.ascontiguousarray(v) for k, v in lay_out(**{k: np.asarray(v) for k, v in inputs.items()}).items()}
    nc = _bacc.Bacc("TRN2", target_bir_lowering=False, num_devices=1)
    dram = {k: nc.dram_tensor(k + "_dram", a.shape, mybir.dt.from_np(a.dtype), kind="ExternalInput").ap()
            for k, a in arrays.items()}
    dram["out"] = nc.dram_tensor("out_dram", (P, KT, LAT), F32, kind="ExternalOutput").ap()
    build(nc, dram)
    r = _run(nc, [{k + "_dram": a for k, a in arrays.items()}], core_ids=[0])
    out = r.results[0]["out_dram"]
    return out.transpose(1, 0, 2).reshape(D, LAT).T.reshape(1, LAT, D)
```
